# Optimizing a Trainium2 kernel written in Bass

```python
import jax, jax.numpy as jnp
from jax import lax
import numpy as np

D_MODEL = 2048
BATCH = 1
SEQ = 256
DEPTH = 1
DEC_BATCH = 8
DEC_SEQ = 1
PAST_LEN = 2048
PAGE_SIZE = 128

D_MIX = D_MODEL
D_HGRN = D_MIX // 2
HGRN_DK = 128
HGRN_DV = 128
HGRN_HEADS = D_HGRN // HGRN_DV
D_FORGET = HGRN_HEADS * HGRN_DK
D_POOL = D_MIX - D_HGRN
POOL_WINDOWS = (2, 4, 8, 16)
N_POOL = len(POOL_WINDOWS)
D_PG = D_POOL // N_POOL
POOL_BUF = max(POOL_WINDOWS) - 1
D_IN = 2 * D_FORGET + 2 * D_HGRN + D_POOL
D_FF = -(-(8 * D_MODEL) // (3 * 256)) * 256
PLE_DIM = 256
CHUNK = 16
EPS = 1e-6

kernel_name = "hymba_hgrn2_multiscale_pool_decoder"

def _rmsnorm(x, g):
    xf = x.astype(jnp.float32)
    y = xf * lax.rsqrt(jnp.mean(xf * xf, axis=-1, keepdims=True) + EPS)
    return (y * g.astype(jnp.float32)).astype(x.dtype)

def _hgrn2_chunked(q, k, v, log_f, S0):
    B, T, H, _ = q.shape
    C = min(CHUNK, T)
    n = -(-T // C)
    pad = n * C - T
    if pad:
        pz = ((0, 0), (0, pad), (0, 0), (0, 0))
        q, k, v, log_f = (jnp.pad(a, pz) for a in (q, k, v, log_f))

    def to_chunks(a):
        return a.reshape(B, n, C, H, a.shape[-1]).transpose(1, 0, 3, 2, 4)

    qc, kc, vc, gc = (to_chunks(a) for a in (q, k, v, log_f))
    mask = jnp.tril(jnp.ones((C, C), dtype=bool))[:, :, None]

    def step(S, inp):
        qb, kb, vb, gb = inp
        b = jnp.cumsum(gb, axis=-2)
        diff = b[..., :, None, :] - b[..., None, :, :]
        decay = jnp.exp(jnp.where(mask, diff, -jnp.inf))
        A = jnp.einsum('bhtd,bhsd,bhtsd->bhts', qb, kb, decay)
        o = (jnp.einsum('bhts,bhsv->bhtv', A, vb)
             + jnp.einsum('bhtd,bhdv->bhtv', qb * jnp.exp(b), S))
        bl = b[..., -1:, :]
        S_new = (jnp.exp(bl[..., 0, :])[..., None] * S
                 + jnp.einsum('bhsd,bhsv->bhdv', kb * jnp.exp(bl - b), vb))
        return S_new, o

    S, o = lax.scan(step, S0, (qc, kc, vc, gc))
    o = o.transpose(1, 0, 3, 2, 4).reshape(B, n * C, H, -1)[:, :T]
    return o, S

def _multiscale_pool(u, buf, start_pos):
    B, T, _ = u.shape
    ext = jnp.concatenate([buf.astype(u.dtype), u], axis=1)
    cs = jnp.cumsum(ext.astype(jnp.float32), axis=1)
    cs = jnp.pad(cs, ((0, 0), (1, 0), (0, 0)))
    pos = start_pos + jnp.arange(T)
    outs = []
    for gi, w in enumerate(POOL_WINDOWS):
        lo, hi = gi * D_PG, (gi + 1) * D_PG
        s = cs[:, POOL_BUF + 1:POOL_BUF + 1 + T, lo:hi] - cs[:, POOL_BUF + 1 - w:POOL_BUF + 1 - w + T, lo:hi]
        cnt = jnp.minimum(pos + 1, w).astype(jnp.float32)
        outs.append(s / cnt[None, :, None])
    mean = jnp.concatenate(outs, axis=-1)
    return mean - u.astype(jnp.float32), ext[:, -POOL_BUF:]

def _layer(h, p_l, S0, buf, start_pos, lb, g_mix, w_in, g_head, w_pool, pool_scale, w_out,
           g_ffn, w_gate_up, w_down, w_ple, g_ple, w_ple_gate):
    B, T, _ = h.shape
    n1 = _rmsnorm(h, g_mix)
    proj = n1 @ w_in
    o1, o2, o3, o4 = D_FORGET, 2 * D_FORGET, 2 * D_FORGET + D_HGRN, 2 * D_FORGET + 2 * D_HGRN
    q_raw, f_raw, v, g_raw, u = proj[..., :o1], proj[..., o1:o2], proj[..., o2:o3], proj[..., o3:o4], proj[..., o4:]

    q = jax.nn.silu(q_raw.astype(jnp.float32)) * (HGRN_DK ** -0.5)
    fg = lb + (1.0 - lb) * jax.nn.sigmoid(f_raw.astype(jnp.float32))
    k = 1.0 - fg
    log_f = jnp.log(fg)
    def heads(a, d):
        return a.reshape(B, T, HGRN_HEADS, d)
    o, S_new = _hgrn2_chunked(heads(q, HGRN_DK), heads(k, HGRN_DK), heads(v.astype(jnp.float32), HGRN_DV),
                              heads(log_f, HGRN_DK), S0.astype(jnp.float32))
    o = _rmsnorm(o, g_head).reshape(B, T, D_HGRN) * jax.nn.silu(g_raw.astype(jnp.float32))

    pooled, buf_new = _multiscale_pool(u, buf, start_pos)
    pm = jnp.einsum('btgc,gcd->btgd', pooled.reshape(B, T, N_POOL, D_PG), w_pool.astype(jnp.float32))
    pm = pm.reshape(B, T, D_POOL) * pool_scale.astype(jnp.float32)

    mix = jnp.concatenate([o, pm], axis=-1).astype(h.dtype)
    h = h + mix @ w_out

    gu = _rmsnorm(h, g_ffn) @ w_gate_up
    h = h + (jax.nn.silu(gu[..., :D_FF]) * gu[..., D_FF:]) @ w_down

    e = _rmsnorm(p_l @ w_ple, g_ple)
    h = h + jax.nn.sigmoid(h @ w_ple_gate) * e
    return h, S_new, buf_new

def _trunk(h, p, S_all, buf_all, start_pos, lbs, g_mix, w_in, g_head, w_pool, pool_scale, w_out,
           g_ffn, w_gate_up, w_down, w_ple, g_ple, w_ple_gate, g_final):
    S_out, buf_out = [], []
    for i in range(DEPTH):
        h, S_i, b_i = _layer(h, p[i], S_all[i], buf_all[i], start_pos, lbs[i], g_mix[i], w_in[i], g_head[i],
                             w_pool[i], pool_scale[i], w_out[i], g_ffn[i], w_gate_up[i], w_down[i],
                             w_ple[i], g_ple[i], w_ple_gate[i])
        S_out.append(S_i)
        buf_out.append(b_i)
    return _rmsnorm(h, g_final), jnp.stack(S_out), jnp.stack(buf_out)

def setup_inputs(seed: int = 0) -> dict:
    key = jax.random.key(seed)
    ks = jax.random.split(key, 20)
    f32 = jnp.float32
    def nrm(k, shape, scale):
        return jax.random.normal(k, shape, f32) * scale
    def gain(k, shape):
        return 1.0 + 0.02 * jax.random.normal(k, shape, f32)
    return {
        'x_prompt': nrm(ks[0], (BATCH, SEQ, D_MODEL), 1.0),
        'x_sample': nrm(ks[1], (DEC_BATCH, DEC_SEQ, D_MODEL), 1.0),
        'state_hgrn': nrm(ks[2], (DEPTH, DEC_BATCH, HGRN_HEADS, HGRN_DK, HGRN_DV), 0.5),
        'state_pool': nrm(ks[3], (DEPTH, DEC_BATCH, POOL_BUF, D_POOL), 1.0),
        'p_prompt': nrm(ks[4], (DEPTH, BATCH, SEQ, PLE_DIM), 1.0),
        'p_sample': nrm(ks[5], (DEPTH, DEC_BATCH, DEC_SEQ, PLE_DIM), 1.0),
        'g_mix': gain(ks[6], (DEPTH, D_MODEL)),
        'w_in': nrm(ks[7], (DEPTH, D_MODEL, D_IN), D_MODEL ** -0.5),
        'lb_logits': nrm(ks[8], (DEPTH, D_FORGET), 0.5),
        'g_head': gain(ks[9], (DEPTH, HGRN_DV)),
        'w_pool': nrm(ks[10], (DEPTH, N_POOL, D_PG, D_PG), D_PG ** -0.5),
        'pool_scale': gain(ks[11], (DEPTH, D_POOL)),
        'w_out': nrm(ks[12], (DEPTH, D_MIX, D_MODEL), D_MIX ** -0.5),
        'g_ffn': gain(ks[13], (DEPTH, D_MODEL)),
        'w_gate_up': nrm(ks[14], (DEPTH, D_MODEL, 2 * D_FF), D_MODEL ** -0.5),
        'w_down': nrm(ks[15], (DEPTH, D_FF, D_MODEL), D_FF ** -0.5),
        'w_ple': nrm(ks[16], (DEPTH, PLE_DIM, D_MODEL), PLE_DIM ** -0.5),
        'g_ple': gain(ks[17], (DEPTH, D_MODEL)),
        'w_ple_gate': nrm(ks[18], (DEPTH, D_MODEL, D_MODEL), D_MODEL ** -0.5),
        'g_final': gain(ks[19], (D_MODEL,)),
    }

def reference(x_prompt, x_sample, state_hgrn, state_pool, p_prompt, p_sample, g_mix, w_in, lb_logits,
              g_head, w_pool, pool_scale, w_out, g_ffn, w_gate_up, w_down, w_ple, g_ple, w_ple_gate, g_final):
    lbs = jnp.cumsum(jax.nn.softmax(lb_logits.astype(jnp.float32), axis=0), axis=0)
    lbs = lbs - lbs[:1]
    weights = (g_mix, w_in, g_head, w_pool, pool_scale, w_out, g_ffn, w_gate_up, w_down,
               w_ple, g_ple, w_ple_gate, g_final)
    S0 = jnp.zeros((DEPTH, BATCH, HGRN_HEADS, HGRN_DK, HGRN_DV), jnp.float32)
    b0 = jnp.zeros((DEPTH, BATCH, POOL_BUF, D_POOL), x_prompt.dtype)
    y_prompt, new_hgrn_prompt, new_pool_prompt = _trunk(x_prompt, p_prompt, S0, b0, 0, lbs, *weights)
    y_sample, new_hgrn_sample, new_pool_sample = _trunk(x_sample, p_sample, state_hgrn, state_pool,
                                                        PAST_LEN, lbs, *weights)
    return (y_prompt, y_sample, new_hgrn_prompt, new_pool_prompt, new_hgrn_sample, new_pool_sample)


_drawn_inputs = setup_inputs


def setup_inputs(seed=0):
    import zlib

    import numpy as np

    out = dict(_drawn_inputs(seed))
    spreads = {}
    factors = {'g_head': 7.106, 'pool_scale': 5.444, 'g_ffn': 4.746, 'g_ple': 7.438, 'g_final': 2.91}
    for name, (base, spread) in spreads.items():
        noise = np.random.default_rng([zlib.crc32(name.encode()), seed]).standard_normal(out[name].shape)
        drawn = base * np.exp(spread * noise) if base else spread * noise
        out[name] = __import__('jax').numpy.asarray(drawn.astype(out[name].dtype))
    for name, factor in factors.items():
        out[name] = (out[name] * factor).astype(out[name].dtype)
    return out
```

```python
from contextlib import ExitStack

import numpy as np

import concourse.bass as bass
from concourse import mybir

ALU = mybir.AluOpType
ACT = mybir.ActivationFunctionType
F32 = mybir.dt.float32
F16 = mybir.dt.float16
U8 = mybir.dt.uint8

P = 128
D = 2048
KT = D // P
SEQ = 256
NSAMP = 8
TOK = SEQ + NSAMP
HEADS = 8
DK = 128
PAIRS = HEADS // 2
WINDOWS = (2, 4, 8, 16)
POOL_BUF = max(WINDOWS) - 1
PLE = 256
DFF = 5632
FT = DFF // P
EPS = 1e-6
LEVELS = 8

COLS = 512
BLOCK_KT = 2
TPG = COLS // P
RAW_SLOTS = 4
HL_SLOTS = 8
AHEAD = 4

WSCALE = 1024.0
NSCALE = 8.0
HSCALE = 0.25
C_N = 1.0 / (WSCALE * NSCALE)
C_FFN = C_N
C_FF = 1.0 / WSCALE
C_H = 1.0 / (WSCALE * HSCALE)
QSCALE = DK ** -0.5

VEC_ROWS = (("g_mix", KT), ("g_ffn", KT), ("g_ple", KT), ("g_final", KT),
            ("pool_scale", 8), ("lb_logits", 8), ("g_head", 1))
VEC_AT = {}
for _name, _n in VEC_ROWS:
    VEC_AT[_name] = (sum(n for _, n in VEC_ROWS[:len(VEC_AT)]), _n)
NVEC = sum(n for _, n in VEC_ROWS)


class Stage:

    def __init__(self, prev, groups, bpg, closed=False, vstep=None, after_pad=False, dmas=1):
        self.dmas = dmas
        self.groups, self.bpg, self.closed, self.after_pad = groups, bpg, closed, after_pad
        self.vstep = vstep or bpg
        self.b0 = prev.b_end if prev else 0
        self.v0 = prev.v_end if prev else 0
        self.t0 = prev.t_end if prev else 0
        self.a0 = prev.a_end if prev else 0
        self.l0 = list(prev.l_end) if prev else [0] * RAW_SLOTS
        self.b_end = self.b0 + groups * bpg
        self.v_end = self.v0 + groups * self.vstep
        closings = groups * (bpg if closed else 1)
        self.t_end = self.t0 + TPG * closings
        self.a_end = self.a0 + (TPG - 1) * closings
        self.per = [sum((self.v0 + j) % RAW_SLOTS == s for j in range(bpg)) for s in range(RAW_SLOTS)]
        self.l_end = [self.l0[s] + groups * self.per[s] * dmas for s in range(RAW_SLOTS)]

    def block(self, i, j):
        return i * self.bpg + (self.b0 + j)

    def raw_slot(self, j):
        return (self.v0 + j) % RAW_SLOTS

    def hl_slot(self, j):
        return (self.v0 + j) % HL_SLOTS

    def landed(self, i, j):
        s = self.raw_slot(j)
        own = sum(self.raw_slot(k) == s for k in range(j + 1))
        return i * (self.per[s] * self.dmas) + (self.l0[s] + own * self.dmas)

    def raw_before(self, j):
        return 2 if self.after_pad and j < 2 else RAW_SLOTS

    def hl_before(self, j):
        return 6 if self.after_pad and j < 6 else HL_SLOTS

    def tile(self, i, n, j=0):
        return (j * TPG if self.closed else i * TPG) + (self.t0 + n)

    def tile_done(self, i, n, j=0):
        if n == TPG - 1:
            return "used", self.block(i, j if self.closed else self.bpg - 1) + 1
        return "acc_done", (j if self.closed else i) * (TPG - 1) + (self.a0 + n + 1)


S_IN = Stage(None, 10, 8)
S_POOL = Stage(S_IN, 1, 2, closed=True)
S_OUT = Stage(S_POOL, 4, 8)
S_PLE = Stage(S_OUT, 1, 4, closed=True)
S_FFN = Stage(S_PLE, DFF // 256, 8, dmas=2)
S_DOWN = Stage(S_FFN, 4, FT // BLOCK_KT, vstep=24, after_pad=True)
S_GATE = Stage(S_DOWN, 4, 8, after_pad=True)
NBLOCKS = S_GATE.b_end
G_MAIN = 6

JOBS = [("vec", "dve")]
JOBS += [(f"n1_{k}", "dve") for k in range(KT)]
JOBS += [(f"pt_{k}", "dve") for k in range(2)]
for _p in range(PAIRS):
    JOBS += [(f"kv_{_p}", "dve"), (f"vt_{_p}", "act")]
    JOBS += [(f"ou_{2 * _p}_0", "dve"), (f"ou_{2 * _p}_1", "dve")]
    JOBS += [(f"lv_{_p}_{l}", "dve") for l in range(LEVELS)]
    JOBS += [(f"cr_{_p}", "act"), (f"ks_{_p}", "act")]
    JOBS += [(f"ou_{2 * _p + 1}_0", "dve"), (f"ou_{2 * _p + 1}_1", "dve")]
    JOBS += [(f"o_{_p}", "act"), (f"sf_{_p}", "act"), (f"os_{_p}", "dve")]
JOBS += [("sb", "dve"), ("ut_0", "act"), ("ut_1", "act"), ("oss", "dve")]
JOBS += [(f"xt_{k}", "dve") for k in range(KT // 2)]
JOBS += [(f"ot_{j}", "dve") for j in range(PAIRS)]
JOBS += [(f"xt_{k}", "dve") for k in range(KT // 2, KT)]
JOBS += [("hs", "dve"), ("es", "dve")]
JOBS += [("ys", "dve")] + [(f"yt_{k}", "act" if k % 2 else "dve") for k in range(KT)]
JOB = {name: n for n, (name, _) in enumerate(JOBS)}
JOB_BANKS = 4


def job_value(name):
    return JOB[name] + 1


def drained_value(n):
    return sum(e == JOBS[n][1] for _, e in JOBS[:n + 1])


def drain_of(name):
    return JOBS[JOB[name]][1], drained_value(JOB[name])


def build(nc, io):
    with ExitStack() as ctx:
        def sb(name, shape, dt=F32):
            return ctx.enter_context(nc.sbuf_tensor(name, shape, dt))

        def sem(name):
            return ctx.enter_context(nc.semaphore(name))

        raw = sb("raw", [P, RAW_SLOTS, BLOCK_KT * COLS])
        hi = sb("hi", [P, HL_SLOTS, BLOCK_KT * COLS], F16)
        lo = sb("lo", [P, HL_SLOTS, BLOCK_KT * COLS], F16)
        nrm = sb("nrm", [P, KT * TOK])
        mix = sb("mix", [P, KT * TOK])
        xe = sb("xe", [P, 3 * D])
        big = sb("big", [P, 6 * HEADS * TOK])
        hid = sb("hid", [P, KT * TOK])

        n_hi = nrm[:, 0:KT * TOK // 2].bitcast(F16).rearrange("p (k t) -> p k t", t=TOK)
        n_lo = nrm[:, KT * TOK // 2:].bitcast(F16).rearrange("p (k t) -> p k t", t=TOK)
        m_hi = mix[:, 0:KT * TOK // 2].bitcast(F16).rearrange("p (k t) -> p k t", t=TOK)
        m_lo = mix[:, KT * TOK // 2:].bitcast(F16).rearrange("p (k t) -> p k t", t=TOK)
        x_tok = xe[:, 0:2 * D].rearrange("p (a d) -> p a d", a=2)
        x_smp = xe[0:NSAMP, 2 * D:3 * D]
        e_all = xe[:, 0:KT * TOK].rearrange("p (k t) -> p k t", t=TOK)
        h_all = hid[:, :].rearrange("p (k t) -> p k t", t=TOK)

        def part(n):
            return big[:, n * HEADS * TOK:(n + 1) * HEADS * TOK].rearrange("p (h t) -> p h t", t=TOK)

        q_all, f_all, k_all, v_all, sg_all, u_all = (part(n) for n in range(6))
        pd_all = v_all
        FFW = FT * TOK // 2
        ff_hi = big[:, 0:FFW].bitcast(F16).rearrange("p (k t) -> p k t", t=TOK)
        ff_lo = big[:, FFW:2 * FFW].bitcast(F16).rearrange("p (k t) -> p k t", t=TOK)
        xn_tok = big[:, 0:2 * D].rearrange("p (a d) -> p a d", a=2)
        xn_smp = big[0:NSAMP, 2 * D:3 * D]
        ple_tok = big[:, 3 * D:3 * D + 2 * PLE].rearrange("p (a d) -> p a d", a=2)
        ple_smp = big[0:NSAMP, 3 * D + 2 * PLE:3 * D + 3 * PLE]
        vec_rows = big[0:NVEC, 3 * D + 3 * PLE:3 * D + 3 * PLE + P]
        junk = big[:, 4 * D:5 * D]
        masks_f = big[:, 5 * D:5 * D + LEVELS * P]
        e_sq = mix[:, :]
        y_tok = big[:, 0:2 * D].rearrange("p (a d) -> p a d", a=2)
        y_smp = big[0:NSAMP, 2 * D:3 * D]
        pd_hi = nrm[:, 0:HEADS * TOK // 2].bitcast(F16).rearrange("p (k t) -> p k t", t=TOK)
        pd_lo = nrm[:, HEADS * TOK // 2:HEADS * TOK].bitcast(F16).rearrange("p (k t) -> p k t", t=TOK)
        lev = mix[:, 0:LEVELS * 2 * SEQ].rearrange("p (l h t) -> p l h t", l=LEVELS, h=2)
        pre = hid[:, 0:512].rearrange("p (h t) -> p h t", h=2)
        suf = hid[:, 512:1024].rearrange("p (h t) -> p h t", h=2)
        k_end = hid[:, 1024:1536].rearrange("p (h t) -> p h t", h=2)
        k_end_tok = hid[:, 512:1024].rearrange("p (h a d) -> p h a d", h=2, a=2)
        v_tok = hid[:, 1536:2048].rearrange("p (h a v) -> p h a v", h=2, a=2)
        buf_tok = hid[0:NSAMP * POOL_BUF, 2048:3072]
        k_mask = hid[0:NSAMP, 3072:4096].rearrange("p (b d) -> p b d", b=NSAMP)

        scores = sb("scores", [P, 3, 2, P])
        kv_smp = sb("kv_smp", [NSAMP, 4, P])
        state = sb("state", [P, 2, NSAMP, P])
        s_final = sb("s_final", [P, 2, P])
        o_tok = sb("o_tok", [P, HEADS, 2, P])
        gate_t = sb("gate_t", [P, TPG, TOK])
        a32 = sb("a32", [P, 2, TOK])
        tg32 = sb("tg32", [P, 2, TOK])
        ident = sb("ident", [P, P])
        ones = sb("ones", [P, P])
        masks = sb("masks", [P, LEVELS, P], U8)
        rcnt = sb("rcnt", [P, 4, 16])
        win_sel = sb("win_sel", [NSAMP * POOL_BUF, 4, NSAMP])
        vec = sb("vec", [P, NVEC])
        gm8 = sb("gm8", [P, KT])
        gf8 = sb("gf8", [P, KT])
        gh8 = sb("gh8", [P, 1])
        ps8 = sb("ps8", [P, 8])
        lbt = sb("lbt", [P, 4, 8])
        nomlb = sb("nomlb", [P, 8])
        ss = sb("ss", [P, 3])
        rs = sb("rs", [P, 3])
        ss_o = sb("ss_o", [P, HEADS, 2])
        rs_o = sb("rs_o", [P, HEADS, 2])
        o_smp = sb("o_smp", [P, HEADS, NSAMP])
        o_sq = sb("o_sq", [P, HEADS, NSAMP])
        pt_hi = sb("pt_hi", [P, 2, TOK], F16)
        pt_lo = sb("pt_lo", [P, 2, TOK], F16)
        u_last = big[0:POOL_BUF + NSAMP, HEADS * TOK:HEADS * TOK + 8 * P]
        win = [mix[:, 3200 + 512 * n:3712 + 512 * n].rearrange("p (h t) -> p h t", h=2) for n in range(2)]
        h_sq, h_ssq = a32[:, 0, :], a32[:, 1, :]
        rstd_bc = gate_t[:, TPG - 1, :]

        acc = ctx.enter_context(nc.psum_tensor("acc", [P, TPG, 512], F32))
        wrk = ctx.enter_context(nc.psum_tensor("wrk", [P, JOB_BANKS, 512], F32))

        landed = [sem(f"landed{s}") for s in range(RAW_SLOTS)]
        hi_done, lo_done, used = sem("hi_done"), sem("lo_done"), sem("used")
        acc_done, acc_free = sem("acc_done"), sem("acc_free")
        gate_ready = sem("gate_ready")
        job_done = sem("job_done")
        drained = {"act": sem("drained_act"), "dve": sem("drained_dve")}
        x_in, c_in, v_in, p_in, buf_in = sem("x_in"), sem("c_in"), sem("v_in"), sem("p_in"), sem("buf_in")
        state_in = [sem("state_in0"), sem("state_in1")]
        state_out = [sem("state_out0"), sem("state_out1")]
        stored, buf_stored = sem("stored"), sem("buf_stored")
        const_ready = sem("const_ready")
        sq_ready, mean_ready, rstd_ready, xn_ready = sem("sq_ready"), sem("mean_ready"), sem("rstd_ready"), sem("xn_ready")
        n_hi_ready, n_ready = sem("n_hi_ready"), sem("n_ready")
        lev_ready, zero_ready, kmask_ready = sem("lev_ready"), sem("zero_ready"), sem("kmask_ready")
        sf_ready, sf_out = sem("sf_ready"), sem("sf_out")
        pool_ready, pd_hi_ready, pd_ready = sem("pool_ready"), sem("pd_hi_ready"), sem("pd_ready")
        mix_tmp, mix_hi, mix_ready = sem("mix_tmp"), sem("mix_hi"), sem("mix_ready")
        ut_ready = sem("ut_ready")
        chain = sem("chain")
        pool_chain = sem("pool_chain")
        esq_ready, esum_ready = sem("esq_ready"), sem("esum_ready")
        out_chain, ffn_chain, down_chain, gate_chain = (sem(n) for n in ("out_chain", "ffn_chain", "down_chain", "gate_chain"))
        osq_ready = sem("osq_ready")
        ff_ready, hg_ready, xn_o = sem("ff_ready"), sem("hg_ready"), sem("xn_o")
        named = {"used": used, "acc_done": acc_done}

        def ntmp(k):
            return (a32, tg32)[k % 4 // 2][:, k % 2, :]

        def y_out(eng, k, scaled):
            name = f"yt_{k}"
            eng.wait_ge(job_done, job_value(name))
            ps, cols = wrk[:, JOB[name] % JOB_BANKS, :], slice(k * P, (k + 1) * P)
            for a in range(2):
                scaled(y_tok[:, a, cols], ps[:, a * P:(a + 1) * P], rs[:, a:a + 1])
            scaled(y_smp[:, cols], ps[0:NSAMP, SEQ:SEQ + P], rs[0:NSAMP, 2:3]).then_inc(drained[JOBS[JOB[name]][1]], 1)

        def wait_tile(eng, st, i, n, j=0):
            name, value = st.tile_done(i, n, j)
            eng.wait_ge(named[name], value)

        def rows(ap):
            return ap.rearrange("o (k p) n -> p (o k) n", p=P)

        w_in, w_out, w_ple, w_down, w_gate = (rows(io[n]) for n in ("w_in", "w_out", "w_ple", "w_down", "w_ple_gate"))
        w_gu = io["w_gate_up"].rearrange("o (k p) (s n) -> p (o k) s n", p=P, s=2)
        w_pool = io["w_pool"].rearrange("o g (k p) n -> p (o g) k n", p=P)

        block = ctx.enter_context(nc.Block())

        @block.sync
        def _(sp):
            def load(st, i, j, src, first=False):
                if not first:
                    sp.wait_ge(lo_done, st.block(i, j) - st.raw_before(j) + 1)
                s = st.raw_slot(j)
                dst = raw[:, s, :]
                if st.dmas == 2:
                    dst = dst.rearrange("p (k s n) -> p k s n", k=BLOCK_KT, s=2)
                    for half in range(2):
                        sp.dma_start(dst[:, :, half, :], src[:, :, half, :]).then_inc(landed[s], 16)
                    return
                if len(src.shape) == 3:
                    dst = dst.rearrange("p (k n) -> p k n", k=src.shape[1])
                elif len(src.shape) == 4:
                    dst = dst.rearrange("p (g k n) -> p g k n", g=src.shape[1], k=src.shape[2])
                sp.dma_start(dst, src).then_inc(landed[s], 16)

            def std(w):
                return lambda i, j: w[:, 2 * j:2 * j + 2, bass.ds(i * COLS, COLS)]

            def gate_up(i, j):
                return w_gu[:, 2 * j:2 * j + 2, :, bass.ds(i * 256, 256)]

            sp.dma_start(x_tok[:, 0, :], io["x_prompt"][0, 0:P, :]).then_inc(x_in, 16)
            sp.dma_start(x_tok[:, 1, :], io["x_prompt"][0, P:SEQ, :]).then_inc(x_in, 16)
            for j in range(8):
                load(S_IN, 0, j, std(w_in)(0, j), first=j < RAW_SLOTS)
            with sp.Fori(1, S_IN.groups) as i:
                for j in range(8):
                    load(S_IN, i, j, std(w_in)(i, j))
            for j in range(2):
                load(S_POOL, 0, j, w_pool[:, 2 * j:2 * j + 2, :, :])
            with sp.Fori(0, S_OUT.groups) as i:
                for j in range(8):
                    load(S_OUT, i, j, std(w_out)(i, j))
            for j in range(4):
                load(S_PLE, 0, j, w_ple[:, :, j * COLS:(j + 1) * COLS])
            with sp.Fori(0, S_FFN.groups) as i:
                for j in range(8):
                    load(S_FFN, i, j, gate_up(i, j))
            with sp.Fori(0, S_DOWN.groups) as i:
                for j in range(S_DOWN.bpg):
                    load(S_DOWN, i, j, std(w_down)(i, j))
            with sp.Fori(0, S_GATE.groups) as i:
                for j in range(8):
                    load(S_GATE, i, j, std(w_gate)(i, j))
            for c in range(4):
                sp.wait_ge(drained["dve"], drain_of(f"yt_{4 * c + 2}")[1])
                sp.wait_ge(drained["act"], drain_of(f"yt_{4 * c + 3}")[1])
                cols = slice(c * COLS, (c + 1) * COLS)
                sp.dma_start(io["y_prompt"][0, :, cols].rearrange("(a p) d -> p a d", p=P), y_tok[:, :, cols])\
                    .then_inc(stored, 16)
                sp.dma_start(io["y_sample"][:, 0, cols], y_smp[:, cols]).then_inc(stored, 16)
            sp.wait_ge(stored, 16 * 8)
            sp.wait_ge(buf_stored, 16 * 3)
            sp.wait_ge(sf_out, 16 * PAIRS)
            sp.wait_ge(state_out[0], 16 * PAIRS)
            sp.wait_ge(state_out[1], 16 * PAIRS)

        @block.gpsimd
        def _(pool):
            links = [0]

            def link(ins):
                links[0] += 1
                ins.then_inc(pool_chain, 1)
                pool.wait_ge(pool_chain, links[0])

            def load_state(h):
                pool.dma_start(state[:, h % 2, :, :], io["state_hgrn"][0, :, h, :, :].rearrange("b d v -> d b v"))\
                    .then_inc(state_in[h % 2], 16)

            load_state(0)
            load_state(1)
            pool.dma_start(buf_tok, io["state_pool"][0].rearrange("b j c -> (b j) c")).then_inc(buf_in, 16)
            pool.dma_start(io["new_pool_sample"][0, :, 0:POOL_BUF - 1, :], io["state_pool"][0, :, 1:POOL_BUF, :])\
                .then_inc(buf_stored, 16)
            for p in range(PAIRS):
                if p:
                    pool.wait_ge(job_done, job_value(f"o_{p - 1}"))
                nc.gpsimd.memset(scores[:, 0:2], 0.0).then_inc(zero_ready, 1)
                for h in (2 * p, 2 * p + 1):
                    if h % 2 == 0:
                        pool.wait_ge(drained["dve"], drain_of(f"kv_{p}")[1])
                        pool.wait_ge(c_in, 16 * 4)
                    if h:
                        pool.wait_ge(job_done, job_value(f"ou_{h - 1}_1"))
                    nc.gpsimd.tensor_tensor(
                        k_mask, kv_smp[:, h % 2, :].unsqueeze(1).to_broadcast([NSAMP, NSAMP, P]),
                        ident[0:NSAMP, 0:NSAMP].unsqueeze(2).to_broadcast([NSAMP, NSAMP, P]),
                        ALU.mult).then_inc(kmask_ready, 1)
                for h in (2 * p, 2 * p + 1):
                    pool.wait_ge(drained["dve"], drain_of(f"ou_{h}_1")[1])
                    pool.dma_start(io["new_hgrn_sample"][0, :, h, :, :].rearrange("b d v -> d b v"),
                                   state[:, h % 2, :, :]).then_inc(state_out[h % 2], 16)
                if p + 1 < PAIRS:
                    pool.wait_ge(job_done, job_value(f"os_{p}"))
                    for h in (2 * p + 2, 2 * p + 3):
                        pool.wait_ge(state_out[h % 2], 16 * (p + 1))
                        load_state(h)
            pool.wait_ge(acc_free, S_IN.t_end)
            pool.wait_ge(job_done, job_value(f"cr_{PAIRS - 1}"))
            for g, w in enumerate(WINDOWS):
                u = u_all[:, 2 * g:2 * g + 2, 0:SEQ]
                pd = pd_all[:, 2 * g:2 * g + 2, 0:SEQ]
                src, m, n = u, 1, 0
                while m < w:
                    dst = win[n % 2]
                    nc.gpsimd.tensor_copy(dst[:, :, 0:m], src[:, :, 0:m])
                    link(nc.gpsimd.tensor_tensor(dst[:, :, m:SEQ], src[:, :, m:SEQ], src[:, :, 0:SEQ - m], ALU.add))
                    src, m, n = dst, 2 * m, n + 1
                nc.gpsimd.tensor_tensor(src[:, :, 0:16], src[:, :, 0:16],
                                        rcnt[:, g, :].unsqueeze(1).to_broadcast([P, 2, 16]), ALU.mult)
                link(nc.gpsimd.tensor_scalar(src[:, :, 16:SEQ], src[:, :, 16:SEQ], 1.0 / w, None, ALU.mult))
                nc.gpsimd.tensor_tensor(pd, src, u, ALU.subtract).then_inc(pool_ready, 1)
                if g < 3:
                    pool.wait_ge(pool_ready, g + 1)
            pool.wait_ge(drained["act"], drain_of("ut_1")[1])
            pool.dma_start(io["new_pool_prompt"][0, 0, :, :], u_last[0:POOL_BUF, :]).then_inc(buf_stored, 16)
            pool.dma_start(io["new_pool_sample"][0, :, POOL_BUF - 1, :], u_last[POOL_BUF:, :]).then_inc(buf_stored, 16)
            pool.wait_ge(esq_ready, 1)
            n = KT // 2
            while n:
                step = nc.gpsimd.tensor_tensor(e_sq[:, 0:n * TOK], e_sq[:, 0:n * TOK], e_sq[:, n * TOK:2 * n * TOK], ALU.add)
                if n > 1:
                    link(step)
                else:
                    step.then_inc(esum_ready, 1)
                n //= 2

        @block.scalar
        def _(act):
            def split(st, i, j):
                act.wait_ge(landed[st.raw_slot(j)], 16 * st.landed(i, j))
                b = st.block(i, j)
                if not (isinstance(b, int) and b < HL_SLOTS):
                    act.wait_ge(used, b - st.hl_before(j) + 1)
                nc.scalar.activation(hi[:, st.hl_slot(j), :], raw[:, st.raw_slot(j), :], ACT.Copy,
                                     scale=WSCALE).then_inc(hi_done, 1)

            def gates(st, i, ns, c, j=0):
                for n in ns:
                    wait_tile(act, st, i, n, j)
                    nc.scalar.activation(gate_t[:, n, :], acc[:, n, 0:TOK], ACT.Sigmoid, scale=c).then_inc(gate_ready, 1)

            def group(st, i, evac, nxt=None):
                for j in range(AHEAD, st.bpg):
                    split(st, i, j)
                if nxt is None:
                    for j in range(AHEAD):
                        split(st, i + 1, j)
                else:
                    for j in range(min(AHEAD, nxt.bpg)):
                        split(nxt, 0, j)
                evac()

            def wait_job(name):
                act.wait_ge(job_done, job_value(name))

            act.dma_start(x_smp, io["x_sample"][:, 0, :]).then_inc(x_in, 16)
            for name, n in VEC_ROWS:
                at = VEC_AT[name][0]
                src = io[name].rearrange("a (k p) -> (a k) p", p=P) if name != "g_final" else \
                    io[name].rearrange("(k p) -> k p", p=P)
                act.dma_start(vec_rows[at:at + n, :], src).then_inc(v_in, 16)
            act.dma_start(ident[:], io["c_ident"]).then_inc(c_in, 16)
            act.dma_start(masks_f, io["c_masks"].rearrange("p l t -> p (l t)")).then_inc(c_in, 16)
            act.dma_start(rcnt[:], io["c_rcnt"]).then_inc(c_in, 16)
            act.dma_start(win_sel[:], io["c_win"]).then_inc(c_in, 16)
            act.dma_start(ple_tok, io["p_prompt"][0, 0].rearrange("(a p) d -> p a d", p=P)).then_inc(p_in, 16)
            act.dma_start(ple_smp, io["p_sample"][0, :, 0, :]).then_inc(p_in, 16)
            act.wait_ge(x_in, 48)
            act.wait_ge(const_ready, 1)
            for a in range(2):
                if a:
                    act.wait_ge(sq_ready, a)
                nc.scalar.activation(junk, x_tok[:, a, :], ACT.Square, accum_out=ss[:, a:a + 1]).then_inc(sq_ready, 1)
            act.wait_ge(sq_ready, 2)
            nc.scalar.activation(junk[0:NSAMP, :], x_smp, ACT.Square, accum_out=ss[0:NSAMP, 2:3]).then_inc(sq_ready, 1)
            act.wait_ge(mean_ready, 1)
            nc.scalar.activation(rs[:], rs[:], ACT.Sqrt).then_inc(rstd_ready, 1)
            act.wait_ge(mean_ready, 2)
            nc.scalar.activation(lbt[:, 1, :], lbt[:, 0, :], ACT.Exp).then_inc(rstd_ready, 1)
            for j in range(AHEAD):
                split(S_IN, 0, j)
            act.wait_ge(const_ready, 2)
            for k in range(KT):
                wait_job(f"n1_{k}")
                nc.scalar.activation(n_hi[:, k, :], wrk[:, JOB[f"n1_{k}"] % JOB_BANKS, 0:TOK], ACT.Copy,
                                     scale=gm8[:, k:k + 1]).then_inc(n_hi_ready, 1)
            group(S_IN, 0, lambda: gates(S_IN, 0, range(TPG), C_N))
            with act.Fori(1, 4) as i:
                group(S_IN, i, lambda: gates(S_IN, i, range(TPG), C_N))
            with act.Fori(4, G_MAIN) as i:
                group(S_IN, i, lambda: None)
            for p in range(PAIRS):
                i = G_MAIN + p
                group(S_IN, i, (lambda: gates(S_IN, i, range(TPG), C_N)) if i < 8 else (lambda: None),
                      S_POOL if i == 9 else None)
                wait_job(f"vt_{p}")
                nc.scalar.activation(v_tok, wrk[:, JOB[f"vt_{p}"] % JOB_BANKS, :].rearrange("p (h a v) -> p h a v", h=2, a=2),
                                     ACT.Copy).then_inc(drained["act"], 1)
                wait_job(f"cr_{p}")
                nc.scalar.activation(scores[:, 2], wrk[:, JOB[f"cr_{p}"] % JOB_BANKS, 0:256].rearrange("p (h t) -> p h t", h=2),
                                     ACT.Copy).then_inc(drained["act"], 1)
                wait_job(f"ks_{p}")
                nc.scalar.activation(k_end_tok, wrk[:, JOB[f"ks_{p}"] % JOB_BANKS, :].rearrange("p (h a v) -> p h a v", h=2, a=2),
                                     ACT.Copy).then_inc(drained["act"], 1)
                wait_job(f"o_{p}")
                o_ps = wrk[:, JOB[f"o_{p}"] % JOB_BANKS, :].rearrange("p (h a v) -> p h a v", h=2, a=2)
                for h in range(2):
                    for a in range(2):
                        nc.scalar.activation(gate_t[:, 2 * h + a, 0:P], o_ps[:, h, a, :], ACT.Square,
                                             accum_out=ss_o[:, 2 * p + h, a:a + 1])
                nc.scalar.activation(o_tok[:, 2 * p:2 * p + 2], o_ps, ACT.Copy).then_inc(drained["act"], 1)
                wait_job(f"sf_{p}")
                if p:
                    act.wait_ge(sf_out, 16 * p)
                nc.scalar.activation(s_final[:], wrk[:, JOB[f"sf_{p}"] % JOB_BANKS, 0:256].rearrange("p (h v) -> p h v", h=2),
                                     ACT.Copy).then_inc(drained["act"], 1)
                act.wait_ge(drained["act"], drain_of(f"sf_{p}")[1])
                act.dma_start(io["new_hgrn_prompt"][0, 0, 2 * p:2 * p + 2].rearrange("h d v -> d h v"), s_final[:])\
                    .then_inc(sf_out, 16)
            act.wait_ge(drained["dve"], drain_of(f"ou_{HEADS - 1}_1")[1])
            for n in range(2):
                wait_job(f"ut_{n}")
                nc.scalar.activation(u_last[:, n * 512:(n + 1) * 512],
                                     wrk[0:POOL_BUF + NSAMP, JOB[f"ut_{n}"] % JOB_BANKS, :], ACT.Copy)\
                    .then_inc(drained["act"], 1)
            act.wait_ge(mean_ready, 3)
            nc.scalar.activation(rs_o[:], rs_o[:], ACT.Sqrt).then_inc(rstd_ready, 1)
            act.wait_ge(mean_ready, 4)
            nc.scalar.activation(o_sq[:], o_sq[:], ACT.Sqrt).then_inc(rstd_ready, 1)
            for j in range(AHEAD):
                split(S_OUT, 0, j)
            for j in range(PAIRS):
                act.wait_ge(mix_tmp, j + 1)
                nc.scalar.activation(m_hi[:, 2 * j:2 * j + 2, 0:SEQ], (a32, tg32)[j % 2][:, :, 0:SEQ], ACT.Copy)\
                    .then_inc(mix_hi, 1)
            act.wait_ge(pool_ready, len(WINDOWS))
            act.wait_ge(pd_ready, 1)
            act.wait_ge(used, S_IN.b_end)
            nc.scalar.activation(pd_hi, pd_all, ACT.Copy, scale=NSCALE).then_inc(pd_hi_ready, 1)
            for j in range(2):
                for n in range(TPG):
                    wait_tile(act, S_POOL, 0, n, j)
                    k = TPG * j + n
                    nc.scalar.activation(m_hi[:, 8 + k, :], acc[:, n, 0:TOK], ACT.Copy, scale=ps8[:, k:k + 1])\
                        .then_inc(mix_hi, 1)
            with act.Fori(0, S_OUT.groups - 1) as i:
                group(S_OUT, i, lambda: None)
            group(S_OUT, S_OUT.groups - 1, lambda: None, S_PLE)
            for j in range(AHEAD):
                split(S_FFN, 0, j)
            act.wait_ge(mean_ready, 5)
            nc.scalar.activation(rstd_bc, rstd_bc, ACT.Sqrt).then_inc(rstd_ready, 1)
            for k in range(KT):
                act.wait_ge(xn_ready, 3 + k + 1)
                nc.scalar.activation(n_hi[:, k, :], ntmp(k), ACT.Copy, scale=gf8[:, k:k + 1]).then_inc(n_hi_ready, 1)
            act.wait_ge(acc_free, S_PLE.t_end)
            nc.scalar.activation(e_sq, xe[:, 0:KT * TOK], ACT.Square).then_inc(esq_ready, 1)
            with act.Fori(0, S_FFN.groups - 1) as i:
                group(S_FFN, i, lambda: gates(S_FFN, i, range(2), C_FFN))
            group(S_FFN, S_FFN.groups - 1, lambda: gates(S_FFN, S_FFN.groups - 1, range(2), C_FFN), S_DOWN)
            act.wait_ge(mean_ready, 6)
            nc.scalar.activation(rstd_bc, rstd_bc, ACT.Sqrt).then_inc(rstd_ready, 1)
            with act.Fori(0, S_DOWN.groups - 1) as i:
                group(S_DOWN, i, lambda: None)
            group(S_DOWN, S_DOWN.groups - 1, lambda: None, S_GATE)
            with act.Fori(0, S_GATE.groups - 1) as i:
                group(S_GATE, i, lambda: gates(S_GATE, i, range(TPG), C_H))
            last = S_GATE.groups - 1
            for j in range(AHEAD, 8):
                split(S_GATE, last, j)
            gates(S_GATE, last, range(TPG), C_H)
            act.wait_ge(mean_ready, 7)
            nc.scalar.activation(rs[:], rs[:], ACT.Sqrt).then_inc(rstd_ready, 1)
            act.wait_ge(rstd_ready, 7)
            for k in range(1, KT, 2):
                y_out(act, k, lambda out, src, scale: nc.scalar.activation(out, src, ACT.Copy, scale=scale))

        @block.vector
        def _(dve):
            links = [0]
            stt, ts, tt = nc.vector.scalar_tensor_tensor, nc.vector.tensor_scalar, nc.vector.tensor_tensor

            def link(ins):
                links[0] += 1
                ins.then_inc(chain, 1)
                dve.wait_ge(chain, links[0])

            def split(st, i, j):
                dve.wait_ge(hi_done, st.block(i, j) + 1)
                stt(lo[:, st.hl_slot(j), :], raw[:, st.raw_slot(j), :], WSCALE, hi[:, st.hl_slot(j), :],
                    ALU.mult, ALU.subtract).then_inc(lo_done, 1)

            def group(st, i, evac, nxt=None, between=None):
                later = [(st, i, j) for j in range(AHEAD, st.bpg)]
                later += [(st, i + 1, j) for j in range(AHEAD)] if nxt is None else \
                    [(nxt, 0, j) for j in range(min(AHEAD, nxt.bpg))]
                for n, s in enumerate(later):
                    split(*s)
                    if between:
                        between(n)
                evac()

            def wait_job(name):
                dve.wait_ge(job_done, job_value(name))

            def drain(ins, name):
                ins.then_inc(drained["dve"], 1)

            def bank(name):
                return wrk[:, JOB[name] % JOB_BANKS, :]

            nc.vector.memset(ones[:], 1.0)
            nc.vector.memset(ss[:], 1.0).then_inc(const_ready, 1)
            wait_job("vec")
            drain(nc.vector.tensor_copy(vec[:], bank("vec")[:, 0:NVEC]), "vec")
            dve.wait_ge(drained["dve"], 1)

            def v(name):
                at, n = VEC_AT[name]
                return vec[:, at:at + n]

            ts(gf8[:], v("g_ffn"), NSCALE, None, ALU.mult)
            ts(gh8[:], v("g_head"), NSCALE, None, ALU.mult)
            ts(ps8[:], v("pool_scale"), NSCALE * C_N, None, ALU.mult)
            ts(gm8[:], v("g_mix"), NSCALE, None, ALU.mult).then_inc(const_ready, 1)
            dve.wait_ge(sq_ready, 3)
            link(ts(rs[:], ss[:], 1.0 / D, EPS, ALU.mult, ALU.add))
            nc.vector.reciprocal(rs[:], rs[:]).then_inc(mean_ready, 1)
            tt(lbt[:, 0, :], v("lb_logits"), v("lb_logits"), ALU.subtract).then_inc(mean_ready, 1)
            dve.wait_ge(rstd_ready, 2)
            dve.wait_ge(x_in, 48)
            ts(xn_tok[:, 0, :], x_tok[:, 0, :], rs[:, 0:1], None, ALU.mult).then_inc(xn_ready, 1)
            ts(xn_tok[:, 1, :], x_tok[:, 1, :], rs[:, 1:2], None, ALU.mult).then_inc(xn_ready, 1)
            ts(xn_smp, x_smp, rs[0:NSAMP, 2:3], None, ALU.mult).then_inc(xn_ready, 1)
            dve.wait_ge(c_in, 64)
            link(nc.vector.tensor_copy(masks[:].rearrange("p l t -> p (l t)"), masks_f))
            link(nc.vector.reciprocal(lbt[:, 2, :], lbt[:, 1, :]))
            link(tt(lbt[:, 2, :], lbt[:, 1, :], lbt[:, 2, :], ALU.mult))
            link(tt(lbt[:, 0, :], lbt[:, 2, :], lbt[:, 2, :], ALU.subtract))
            link(ts(lbt[:, 3, :], lbt[:, 0, :], -1.0, 1.0, ALU.mult, ALU.add))
            ts(nomlb[:], lbt[:, 3, :], -1.0, None, ALU.mult)
            for j in range(AHEAD):
                split(S_IN, 0, j)
            for k in range(KT):
                dve.wait_ge(n_hi_ready, k + 1)
                drain(stt(n_lo[:, k, :], bank(f"n1_{k}")[:, 0:TOK], gm8[:, k:k + 1], n_hi[:, k, :],
                          ALU.mult, ALU.subtract), f"n1_{k}")
            for k in range(2):
                wait_job(f"pt_{k}")
                link(ts(pt_hi[:, k, :], bank(f"pt_{k}")[:, 0:TOK], NSCALE, None, ALU.mult))
                drain(stt(pt_lo[:, k, :], bank(f"pt_{k}")[:, 0:TOK], NSCALE, pt_hi[:, k, :],
                          ALU.mult, ALU.subtract), f"pt_{k}")

            def one(x, i, n=0):
                return x[:, bass.ds(i * TPG + n, 1)]

            def tile_of(x, i, n):
                return one(x, i, n).rearrange("p a t -> p (a t)")

            def evac_q(i):
                for n in range(TPG):
                    dve.wait_ge(gate_ready, i * TPG + (n + 1))
                    stt(tile_of(q_all, i, n), acc[:, n, 0:TOK], C_N * QSCALE, gate_t[:, n, :],
                        ALU.mult, ALU.mult).then_inc(acc_free, 1)

            def evac_f(i):
                for n in range(TPG):
                    dve.wait_ge(gate_ready, i * TPG + (n + 1))
                    ts(tile_of(f_all, i - 2, n), gate_t[:, n, :], one(lbt[:, 3, :], i - 2, n),
                       one(lbt[:, 0, :], i - 2, n), ALU.mult, ALU.add)
                    ts(tile_of(k_all, i - 2, n), gate_t[:, n, :], one(nomlb, i - 2, n),
                       one(lbt[:, 3, :], i - 2, n), ALU.mult, ALU.add).then_inc(acc_free, 1)

            def evac_copy(dst, i, i0):
                for n in range(TPG):
                    wait_tile(dve, S_IN, i, n)
                    ts(tile_of(dst, i - i0, n), acc[:, n, 0:TOK], C_N, None, ALU.mult).then_inc(acc_free, 1)

            def evac_g(i):
                for n in range(TPG):
                    dve.wait_ge(gate_ready, 4 * TPG + (i - 6) * TPG + (n + 1))
                    stt(tile_of(sg_all, i - 6, n), acc[:, n, 0:TOK], C_N, gate_t[:, n, :],
                        ALU.mult, ALU.mult).then_inc(acc_free, 1)

            with dve.Fori(0, 2) as i:
                group(S_IN, i, lambda: evac_q(i))
            with dve.Fori(2, 4) as i:
                group(S_IN, i, lambda: evac_f(i))
            with dve.Fori(4, 6) as i:
                group(S_IN, i, lambda: evac_copy(v_all, i, 4))

            def halves(x, l):
                return x.rearrange("p h (n s k) -> p h n s k", s=2, k=1 << l)

            def level(p, l):
                hs = slice(2 * p, 2 * p + 2)
                q, k, f = (halves(x[:, hs, 0:SEQ], l) for x in (q_all, k_all, f_all))
                x, a, b = halves(lev[:, l], l), halves(pre, l), halves(suf, l)
                size = 1 << l
                shape = [P, 2, SEQ // (2 * size), size]
                if l == 0:
                    if p == 0:
                        dve.wait_ge(acc_free, 4 * TPG)
                    else:
                        wait_job(f"os_{p - 1}")
                    tt(x[:, :, :, 1], q[:, :, :, 1], f[:, :, :, 1], ALU.mult).then_inc(lev_ready, 1)
                    nc.vector.tensor_copy(x[:, :, :, 0], k[:, :, :, 0]).then_inc(lev_ready, 1)
                    nc.vector.memset(b[:, :, :, 1], 1.0)
                    nc.vector.tensor_copy(b[:, :, :, 0], f[:, :, :, 1])
                    nc.vector.tensor_copy(a[:, :, :, 0], f[:, :, :, 0])
                    link(tt(a[:, :, :, 1], f[:, :, :, 1], f[:, :, :, 0], ALU.mult))
                    return
                left_all = a[:, :, :, 0, size - 1:size].to_broadcast(shape)
                right_all = a[:, :, :, 1, size - 1:size].to_broadcast(shape)
                tt(x[:, :, :, 1], q[:, :, :, 1], a[:, :, :, 1], ALU.mult).then_inc(lev_ready, 1)
                tt(x[:, :, :, 0], k[:, :, :, 0], b[:, :, :, 0], ALU.mult).then_inc(lev_ready, 1)
                dve.wait_ge(lev_ready, 17 * p + 2 * l + 2)
                link(tt(b[:, :, :, 0], b[:, :, :, 0], right_all, ALU.mult))
                if l < LEVELS - 1:
                    link(tt(a[:, :, :, 1], a[:, :, :, 1], left_all, ALU.mult))
                else:
                    tt(k_end, k_all[:, hs, 0:SEQ], suf, ALU.mult).then_inc(lev_ready, 1)

            def head_states(h):
                dve.wait_ge(state_in[h % 2], 16 * (h // 2 + 1))
                for j in range(2):
                    name = f"ou_{h}_{j}"
                    wait_job(name)
                    for bb in range(4):
                        b = 4 * j + bb
                        s = state[:, h % 2, b, :]
                        last = stt(s, s, f_all[:, h, SEQ + b:SEQ + b + 1], bank(name)[:, bb * P:(bb + 1) * P],
                                   ALU.mult, ALU.add)
                    drain(last, name)

            for p in range(PAIRS):
                i = G_MAIN + p
                group(S_IN, i, (lambda: evac_g(i)) if i < 8 else (lambda: evac_copy(u_all, i, 8)),
                      S_POOL if i == 9 else None, lambda l: level(p, l))
                if i == 9:
                    for l in range(AHEAD + 2, LEVELS):
                        level(p, l)
                wait_job(f"kv_{p}")
                drain(nc.vector.tensor_copy(kv_smp[:], bank(f"kv_{p}")[0:NSAMP, :].rearrange("p (a d) -> p a d", a=4)),
                      f"kv_{p}")
                head_states(2 * p)
                dve.wait_ge(zero_ready, p + 1)
                for l in range(LEVELS):
                    name = f"lv_{p}_{l}"
                    wait_job(name)
                    if l:
                        dve.wait_ge(drained["dve"], drain_of(f"lv_{p}_{l - 1}")[1])
                    drain(nc.vector.copy_predicated(
                        scores[:, 0:2].rearrange("p a h t -> p (a h) t"),
                        masks[:, l, :].unsqueeze(1).to_broadcast([P, 4, P]),
                        bank(name).rearrange("p (a t) -> p a t", a=4)), name)
                head_states(2 * p + 1)
                wait_job(f"os_{p}")
                drain(nc.vector.tensor_copy(o_smp[:, 2 * p:2 * p + 2, :],
                                            bank(f"os_{p}")[:, 0:16].rearrange("p (h b) -> p h b", h=2)), f"os_{p}")

            dve.wait_ge(drained["dve"], drain_of(f"os_{PAIRS - 1}")[1])
            tt(o_sq[:], o_smp[:], o_smp[:], ALU.mult).then_inc(osq_ready, 1)
            dve.wait_ge(drained["act"], drain_of(f"o_{PAIRS - 1}")[1])
            link(ts(rs_o[:], ss_o[:], 1.0 / P, EPS, ALU.mult, ALU.add))
            nc.vector.reciprocal(rs_o[:], rs_o[:]).then_inc(mean_ready, 1)
            wait_job("sb")
            u_s = u_all[:, :, SEQ:TOK]
            drain(tt(pd_all[:, :, SEQ:TOK], bank("sb")[:, 0:64].rearrange("p (k b) -> p k b", b=NSAMP), u_s, ALU.add), "sb")
            dve.wait_ge(drained["dve"], drain_of("sb")[1])
            for g, w in enumerate(WINDOWS):
                s = slice(2 * g, 2 * g + 2)
                last = stt(pd_all[:, s, SEQ:TOK], pd_all[:, s, SEQ:TOK], 1.0 / w, u_all[:, s, SEQ:TOK],
                           ALU.mult, ALU.subtract)
            last.then_inc(pd_ready, 1)
            wait_job("oss")
            o_sq2 = o_sq[:].rearrange("p h b -> p (h b)")
            link(ts(o_sq2, bank("oss")[:, 0:64], 1.0 / P, EPS, ALU.mult, ALU.add))
            drain(nc.vector.reciprocal(o_sq[:], o_sq[:]), "oss")
            dve.wait_ge(drained["dve"], drain_of("oss")[1])
            nc.vector.tensor_copy(ss[:, 0:1], ss[:, 0:1]).then_inc(mean_ready, 1)
            dve.wait_ge(rstd_ready, 3)
            for h in range(HEADS):
                for a in range(2):
                    ts(o_tok[:, h, a, :], o_tok[:, h, a, :], rs_o[:, h, a:a + 1], None, ALU.mult).then_inc(xn_o, 1)
            dve.wait_ge(rstd_ready, 4)
            link(tt(o_smp[:], o_smp[:], o_sq[:], ALU.mult))
            link(stt(o_smp[:], o_smp[:], gh8[:, 0:1], sg_all[:, :, SEQ:TOK], ALU.mult, ALU.mult))
            link(nc.vector.tensor_copy(m_hi[:, 0:HEADS, SEQ:TOK], o_smp[:]))
            tt(m_lo[:, 0:HEADS, SEQ:TOK], o_smp[:], m_hi[:, 0:HEADS, SEQ:TOK], ALU.subtract).then_inc(mix_ready, 1)

            def x_tile(k):
                wait_job(f"xt_{k}")
                drain(nc.vector.tensor_copy(h_all[:, k, :], bank(f"xt_{k}")[:, 0:TOK]), f"xt_{k}")

            for k in range(KT // 2):
                x_tile(k)
            for j in range(PAIRS):
                name = f"ot_{j}"
                tmp = (a32, tg32)[j % 2][:, :, 0:SEQ]
                wait_job(name)
                stt(tmp, bank(name).rearrange("p (h t) -> p h t", h=2), gh8[:, 0:1],
                    sg_all[:, 2 * j:2 * j + 2, 0:SEQ], ALU.mult, ALU.mult).then_inc(mix_tmp, 1)
                dve.wait_ge(mix_tmp, j + 1)
                dve.wait_ge(mix_hi, j + 1)
                drain(tt(m_lo[:, 2 * j:2 * j + 2, 0:SEQ], tmp, m_hi[:, 2 * j:2 * j + 2, 0:SEQ], ALU.subtract), name)
            for k in range(KT // 2, KT):
                x_tile(k)
            for j in range(AHEAD):
                split(S_OUT, 0, j)
            dve.wait_ge(pd_hi_ready, 1)
            stt(pd_lo, pd_all, NSCALE, pd_hi, ALU.mult, ALU.subtract).then_inc(pd_ready, 1)
            for j in range(2):
                for n in range(TPG):
                    k = TPG * j + n
                    dve.wait_ge(mix_hi, PAIRS + k + 1)
                    stt(m_lo[:, 8 + k, :], acc[:, n, 0:TOK], ps8[:, k:k + 1], m_hi[:, 8 + k, :],
                        ALU.mult, ALU.subtract).then_inc(acc_free, 1)
            nc.vector.memset(h_ssq, 0.0)

            def evac_out(i):
                for n in range(TPG):
                    wait_tile(dve, S_OUT, i, n)
                    h = tile_of(h_all, i, n)
                    stt(h, acc[:, n, 0:TOK], C_N, h, ALU.mult, ALU.add).then_inc(acc_free, 1)
                    dve.wait_ge(acc_free, S_OUT.tile(i, n) + 1)
                    tt(h_sq, h, h, ALU.mult).then_inc(out_chain, 1)
                    dve.wait_ge(out_chain, (i * TPG + n) * 2 + 1)
                    tt(h_ssq, h_ssq, h_sq, ALU.add).then_inc(out_chain, 1)

            with dve.Fori(0, S_OUT.groups - 1) as i:
                group(S_OUT, i, lambda: evac_out(i))
            last_out = S_OUT.groups - 1
            group(S_OUT, last_out, lambda: evac_out(last_out), S_PLE)
            for j in range(4):
                split(S_FFN, 0, j)
                for n in range(TPG):
                    wait_tile(dve, S_PLE, 0, n, j)
                    ts(e_all[:, TPG * j + n, :], acc[:, n, 0:TOK], C_N, None, ALU.mult).then_inc(acc_free, 1)
            wait_job("hs")
            link(ts(rstd_bc, bank("hs")[:, 0:TOK], 1.0 / D, EPS, ALU.mult, ALU.add))
            drain(nc.vector.reciprocal(rstd_bc, rstd_bc), "hs")
            dve.wait_ge(drained["dve"], drain_of("hs")[1])
            nc.vector.tensor_copy(ss[:, 0:1], ss[:, 0:1]).then_inc(mean_ready, 1)
            dve.wait_ge(rstd_ready, 5)
            for k in range(KT + 2):
                if k < KT:
                    if k >= 4:
                        dve.wait_ge(n_ready, k - 3)
                    tt(ntmp(k), h_all[:, k, :], rstd_bc, ALU.mult).then_inc(xn_ready, 1)
                if k >= 2:
                    dve.wait_ge(n_hi_ready, KT + k - 1)
                    stt(n_lo[:, k - 2, :], ntmp(k - 2), gf8[:, k - 2:k - 1], n_hi[:, k - 2, :],
                        ALU.mult, ALU.subtract).then_inc(n_ready, 1)

            def evac_ffn(i):
                for n in range(2):
                    dve.wait_ge(gate_ready, i * 2 + (24 + n + 1))
                    stt(tg32[:, n, :], acc[:, n, 0:TOK], C_FFN, gate_t[:, n, :], ALU.mult, ALU.mult).then_inc(acc_free, 1)
                dve.wait_ge(acc_free, S_FFN.tile(i, 2))
                for n in range(2):
                    wait_tile(dve, S_FFN, i, 2 + n)
                    stt(a32[:, n, :], acc[:, 2 + n, 0:TOK], C_FFN, tg32[:, n, :], ALU.mult, ALU.mult).then_inc(acc_free, 1)
                dve.wait_ge(acc_free, S_FFN.tile(i, 4))
                fh = ff_hi[:, bass.ds(i * 2, 2), :]
                ts(fh, a32[:], 1.0, None, ALU.mult).then_inc(ffn_chain, 1)
                dve.wait_ge(ffn_chain, i + 1)
                tt(ff_lo[:, bass.ds(i * 2, 2), :], a32[:], fh, ALU.subtract).then_inc(ff_ready, 1)

            dve.wait_ge(buf_stored, 16 * 3)
            with dve.Fori(0, S_FFN.groups - 1) as i:
                group(S_FFN, i, lambda: evac_ffn(i))
            group(S_FFN, S_FFN.groups - 1, lambda: evac_ffn(S_FFN.groups - 1), S_DOWN)
            wait_job("es")
            link(ts(rstd_bc, bank("es")[:, 0:TOK], 1.0 / D, EPS, ALU.mult, ALU.add))
            drain(nc.vector.reciprocal(rstd_bc, rstd_bc), "es")
            dve.wait_ge(drained["dve"], drain_of("es")[1])
            nc.vector.tensor_copy(ss[:, 0:1], ss[:, 0:1]).then_inc(mean_ready, 1)
            dve.wait_ge(rstd_ready, 6)
            gp = VEC_AT["g_ple"][0]
            for k in range(KT):
                last = stt(e_all[:, k, :], e_all[:, k, :], vec[:, gp + k:gp + k + 1], rstd_bc, ALU.mult, ALU.mult)
            link(last)
            nc.vector.memset(h_ssq, 0.0)

            def evac_down(i):
                for n in range(TPG):
                    wait_tile(dve, S_DOWN, i, n)
                    h, nh = tile_of(h_all, i, n), tile_of(n_hi, i, n)
                    stt(h, acc[:, n, 0:TOK], C_FF, h, ALU.mult, ALU.add).then_inc(acc_free, 1)
                    dve.wait_ge(acc_free, S_DOWN.tile(i, n) + 1)
                    ts(nh, h, HSCALE, None, ALU.mult).then_inc(down_chain, 1)
                    dve.wait_ge(down_chain, i * TPG + (n + 1))
                    stt(tile_of(n_lo, i, n), h, HSCALE, nh, ALU.mult, ALU.subtract).then_inc(n_ready, 1)

            with dve.Fori(0, S_DOWN.groups - 1) as i:
                group(S_DOWN, i, lambda: evac_down(i))
            last_down = S_DOWN.groups - 1
            group(S_DOWN, last_down, lambda: evac_down(last_down), S_GATE)

            def evac_gate(i):
                for n in range(TPG):
                    dve.wait_ge(gate_ready, i * TPG + (68 + n + 1))
                    h = tile_of(h_all, i, n)
                    tt(tg32[:, 0, :], gate_t[:, n, :], tile_of(e_all, i, n), ALU.mult).then_inc(acc_free, 1)
                    dve.wait_ge(acc_free, S_GATE.tile(i, n) + 1)
                    tt(h, h, tg32[:, 0, :], ALU.add).then_inc(gate_chain, 1)
                    dve.wait_ge(gate_chain, (i * TPG + n) * 3 + 1)
                    tt(h_sq, h, h, ALU.mult).then_inc(gate_chain, 1)
                    dve.wait_ge(gate_chain, (i * TPG + n) * 3 + 2)
                    tt(h_ssq, h_ssq, h_sq, ALU.add).then_inc(gate_chain, 1)

            with dve.Fori(0, S_GATE.groups - 1) as i:
                group(S_GATE, i, lambda: evac_gate(i))
            last_gate = S_GATE.groups - 1
            for j in range(AHEAD, 8):
                split(S_GATE, last_gate, j)
            evac_gate(last_gate)
            dve.wait_ge(gate_chain, KT * 3)
            gf = VEC_AT["g_final"][0]
            for k in range(KT):
                ts(h_all[:, k, :], h_all[:, k, :], vec[:, gf + k:gf + k + 1], None, ALU.mult).then_inc(hg_ready, 1)
            wait_job("ys")
            link(nc.vector.memset(rs[:], 1.0))
            link(ts(rs[:, 0:2], bank("ys")[:, 0:2], 1.0 / D, EPS, ALU.mult, ALU.add))
            link(ts(rs[0:NSAMP, 2:3], bank("ys")[0:NSAMP, 2:3], 1.0 / D, EPS, ALU.mult, ALU.add))
            drain(nc.vector.reciprocal(rs[:], rs[:]), "ys")
            dve.wait_ge(drained["dve"], drain_of("ys")[1])
            nc.vector.tensor_copy(ss[:, 0:1], ss[:, 0:1]).then_inc(mean_ready, 1)
            dve.wait_ge(rstd_ready, 7)
            for k in range(0, KT, 2):
                y_out(dve, k, lambda out, src, scale: ts(out, src, scale, None, ALU.mult))

        @block.tensor
        def _(pe):
            mm = nc.tensor.matmul

            def stream(st, i, x_hi, x_lo, ready=None, layout=None):
                for j in range(st.bpg):
                    pe.wait_ge(lo_done, st.block(i, j) + 1)
                    if ready:
                        ready(j)
                    for n in range(TPG):
                        if j == 0 or st.closed:
                            t = st.tile(i, n, j)
                            if not (isinstance(t, int) and t < TPG):
                                pe.wait_ge(acc_free, t - (TPG - 1))
                        out = acc[:, n, 0:TOK]
                        for kk in range(BLOCK_KT):
                            at, kt = layout(j, n, kk) if layout else (kk * COLS + n * P, BLOCK_KT * j + kk)
                            wh = hi[:, st.hl_slot(j), at:at + P]
                            wl = lo[:, st.hl_slot(j), at:at + P]
                            first = kk == 0 and (j == 0 or st.closed)
                            final = kk == BLOCK_KT - 1 and (j == st.bpg - 1 or st.closed)
                            mm(out, wh, x_hi[:, kt, :], start=first, stop=False)
                            mm(out, wh, x_lo[:, kt, :], start=False, stop=False)
                            last = mm(out, wl, x_hi[:, kt, :], start=False, stop=final)
                        if n == TPG - 1:
                            last.then_inc(used, 1)
                        elif final:
                            last.then_inc(acc_done, 1)

            def job(name):
                n = JOB[name]
                if n >= JOB_BANKS:
                    pe.wait_ge(drained[JOBS[n - JOB_BANKS][1]], drained_value(n - JOB_BANKS))
                return wrk[:, n % JOB_BANKS, :]

            def tokens_to_features(out, src, smp, k):
                for a in range(2):
                    nc.tensor.transpose(out[:, a * P:(a + 1) * P], src[:, a, k * P:(k + 1) * P], ident[:])
                return nc.tensor.transpose(out[:, SEQ:TOK], smp[:, k * P:(k + 1) * P], ident[0:NSAMP, 0:NSAMP])

            pe.wait_ge(c_in, 64)
            pe.wait_ge(v_in, 16 * len(VEC_ROWS))
            nc.tensor.transpose(job("vec")[:, 0:NVEC], vec_rows, ident[0:NVEC, 0:NVEC]).then_inc(job_done, 1)
            pe.wait_ge(xn_ready, 3)
            for k in range(KT):
                tokens_to_features(job(f"n1_{k}"), xn_tok, xn_smp, k).then_inc(job_done, 1)
            pe.wait_ge(p_in, 32)
            for k in range(2):
                tokens_to_features(job(f"pt_{k}"), ple_tok, ple_smp, k).then_inc(job_done, 1)
            pe.wait_ge(drained["dve"], drain_of(f"n1_{KT - 1}")[1])
            stream(S_IN, 0, n_hi, n_lo)
            with pe.Fori(1, G_MAIN) as i:
                stream(S_IN, i, n_hi, n_lo)
            for p in range(PAIRS):
                stream(S_IN, G_MAIN + p, n_hi, n_lo)
                pair = (2 * p, 2 * p + 1)
                out = job(f"kv_{p}")
                for n, src in enumerate((k_all, k_all, v_all, v_all)):
                    last = nc.tensor.transpose(out[0:NSAMP, n * P:(n + 1) * P], src[:, pair[n % 2], SEQ:TOK], ident[:])
                last.then_inc(job_done, 1)
                out = job(f"vt_{p}")
                for n in range(4):
                    last = nc.tensor.transpose(out[:, n * P:(n + 1) * P],
                                               v_all[:, pair[n // 2], (n % 2) * P:(n % 2 + 1) * P], ident[:])
                last.then_inc(job_done, 1)

                def outer(h):
                    pe.wait_ge(kmask_ready, h + 1)
                    for j in range(2):
                        out = job(f"ou_{h}_{j}")
                        for bb in range(4):
                            last = mm(out[:, bb * P:(bb + 1) * P], k_mask[:, 4 * j + bb, :], kv_smp[:, 2 + h % 2, :],
                                      start=True, stop=True)
                        last.then_inc(job_done, 1)

                outer(2 * p)
                for l in range(LEVELS):
                    out = job(f"lv_{p}_{l}")
                    if l:
                        pe.wait_ge(lev_ready, 17 * p + 2 * l)
                    for a in range(2):
                        for h in range(2):
                            s = slice(a * P, (a + 1) * P)
                            lhs = lev[:, l - 1, h, s] if l else k_all[:, pair[h], s]
                            rhs = lev[:, l - 1, h, s] if l else q_all[:, pair[h], s]
                            n = 2 * a + h
                            last = mm(out[:, n * P:(n + 1) * P], lhs, rhs, start=True, stop=True)
                    last.then_inc(job_done, 1)
                pe.wait_ge(lev_ready, 17 * p + 16)
                out = job(f"cr_{p}")
                for h in range(2):
                    last = mm(out[:, h * P:(h + 1) * P], lev[:, LEVELS - 1, h, 0:P], lev[:, LEVELS - 1, h, P:SEQ],
                              start=True, stop=True)
                last.then_inc(job_done, 1)
                pe.wait_ge(lev_ready, 17 * p + 17)
                out = job(f"ks_{p}")
                for n in range(4):
                    last = nc.tensor.transpose(out[:, n * P:(n + 1) * P], k_end[:, n // 2, (n % 2) * P:(n % 2 + 1) * P],
                                               ident[:])
                last.then_inc(job_done, 1)
                outer(2 * p + 1)
                out = job(f"o_{p}")
                pe.wait_ge(drained["dve"], drain_of(f"lv_{p}_{LEVELS - 1}")[1])
                pe.wait_ge(drained["act"], drain_of(f"ks_{p}")[1])
                for h in range(2):
                    mm(out[:, 2 * h * P:(2 * h + 1) * P], scores[:, 0, h, :], v_tok[:, h, 0, :], start=True, stop=True)
                    o1 = out[:, (2 * h + 1) * P:(2 * h + 2) * P]
                    mm(o1, scores[:, 2, h, :], v_tok[:, h, 0, :], start=True, stop=False)
                    last = mm(o1, scores[:, 1, h, :], v_tok[:, h, 1, :], start=False, stop=True)
                last.then_inc(job_done, 1)
                out = job(f"sf_{p}")
                for h in range(2):
                    mm(out[:, h * P:(h + 1) * P], k_end_tok[:, h, 0, :], v_tok[:, h, 0, :], start=True, stop=False)
                    last = mm(out[:, h * P:(h + 1) * P], k_end_tok[:, h, 1, :], v_tok[:, h, 1, :], start=False, stop=True)
                last.then_inc(job_done, 1)
                out = job(f"os_{p}")
                pe.wait_ge(drained["dve"], drain_of(f"ou_{2 * p + 1}_1")[1])
                for h in range(2):
                    for b in range(NSAMP):
                        n = h * NSAMP + b
                        last = mm(out[:, n:n + 1], state[:, h, b, :], q_all[:, pair[h], SEQ + b:SEQ + b + 1],
                                  start=True, stop=True)
                last.then_inc(job_done, 1)
            pe.wait_ge(buf_in, 16)
            out = job("sb")
            for k in range(8):
                last = mm(out[:, k * NSAMP:(k + 1) * NSAMP], buf_tok[:, k * P:(k + 1) * P], win_sel[:, k // 2, :],
                          start=True, stop=True)
            last.then_inc(job_done, 1)
            pe.wait_ge(acc_free, S_IN.t_end)
            for n in range(2):
                out = job(f"ut_{n}")
                for k in range(4):
                    last = nc.tensor.transpose(out[0:POOL_BUF + NSAMP, k * P:(k + 1) * P],
                                               u_all[:, 4 * n + k, SEQ - POOL_BUF:TOK], ident[:])
                last.then_inc(job_done, 1)
            out = job("oss")
            pe.wait_ge(osq_ready, 1)
            mm(out[:, 0:64], ones[:], o_sq[:].rearrange("p h b -> p (h b)"), start=True, stop=True).then_inc(job_done, 1)
            for k in range(KT // 2):
                tokens_to_features(job(f"xt_{k}"), x_tok, x_smp, k).then_inc(job_done, 1)
            for j in range(PAIRS):
                out = job(f"ot_{j}")
                pe.wait_ge(xn_o, 4 * (j + 1))
                for n in range(4):
                    last = nc.tensor.transpose(out[:, n * P:(n + 1) * P], o_tok[:, 2 * j + n // 2, n % 2, :], ident[:])
                last.then_inc(job_done, 1)
            for k in range(KT // 2, KT):
                tokens_to_features(job(f"xt_{k}"), x_tok, x_smp, k).then_inc(job_done, 1)

            pe.wait_ge(pd_ready, 2)
            stream(S_POOL, 0, pd_hi, pd_lo,
                   layout=lambda j, n, kk: ((n // 2 * 2 + kk) * 256 + n % 2 * P, 2 * (2 * j + n // 2) + kk))

            def mix_wait(j):
                if j == 0:
                    pe.wait_ge(drained["dve"], drain_of("xt_15")[1])
                    pe.wait_ge(mix_ready, 1)
                if j >= 4:
                    pe.wait_ge(acc_free, S_POOL.t0 + 2 * (j - 3))
            with pe.Fori(0, S_OUT.groups) as i:
                stream(S_OUT, i, m_hi, m_lo, ready=mix_wait)
            stream(S_PLE, 0, pt_hi, pt_lo, layout=lambda j, n, kk: (kk * COLS + n * P, kk))
            out = job("hs")
            pe.wait_ge(out_chain, 2 * KT)
            mm(out[:, 0:TOK], ones[:], h_ssq, start=True, stop=True).then_inc(job_done, 1)
            with pe.Fori(0, S_FFN.groups) as i:
                stream(S_FFN, i, n_hi, n_lo, ready=lambda j: pe.wait_ge(n_ready, 2 * j + 2))
            out = job("es")
            pe.wait_ge(esum_ready, 1)
            mm(out[:, 0:TOK], ones[:], e_sq[:, 0:TOK], start=True, stop=True).then_inc(job_done, 1)
            with pe.Fori(0, S_DOWN.groups) as i:
                stream(S_DOWN, i, ff_hi, ff_lo, ready=lambda j: pe.wait_ge(ff_ready, j + 1))
            with pe.Fori(0, S_GATE.groups) as i:
                stream(S_GATE, i, n_hi, n_lo, ready=lambda j: pe.wait_ge(n_ready, KT + 2 * j + 2))
            out = job("ys")
            pe.wait_ge(gate_chain, KT * 3)
            for n in range(3):
                m = P if n < 2 else NSAMP
                last = mm(out[0:m, n:n + 1], h_ssq[:, n * P:n * P + m], ones[:, 0:1], start=True, stop=True)
            last.then_inc(job_done, 1)
            for k in range(KT):
                out = job(f"yt_{k}")
                pe.wait_ge(hg_ready, k + 1)
                for a in range(2):
                    nc.tensor.transpose(out[:, a * P:(a + 1) * P], h_all[:, k, a * P:(a + 1) * P], ident[:])
                nc.tensor.transpose(out[0:NSAMP, SEQ:SEQ + P], h_all[:, k, SEQ:TOK], ident[:]).then_inc(job_done, 1)


_INS = ["x_prompt", "x_sample", "state_hgrn", "state_pool", "p_prompt", "p_sample", "g_mix", "w_in", "lb_logits",
        "g_head", "w_pool", "pool_scale", "w_out", "g_ffn", "w_gate_up", "w_down", "w_ple", "g_ple", "w_ple_gate",
        "g_final"]
_OUTS = [("y_prompt", (1, SEQ, D)), ("y_sample", (NSAMP, 1, D)), ("new_hgrn_prompt", (1, 1, HEADS, DK, P)),
         ("new_pool_prompt", (1, 1, POOL_BUF, 1024)), ("new_hgrn_sample", (1, NSAMP, HEADS, DK, P)),
         ("new_pool_sample", (1, NSAMP, POOL_BUF, 1024))]


def _constants():
    s, t = np.arange(P)[:, None], np.arange(P)[None, :]
    masks = np.zeros((P, LEVELS, P), np.float32)
    masks[:, 0] = s == t
    for l in range(LEVELS - 1):
        masks[:, l + 1] = (s >> (l + 1) == t >> (l + 1)) & ((s >> l) % 2 == 0) & ((t >> l) % 2 == 1)
    rcnt = np.zeros((P, 4, 16), np.float32)
    win = np.zeros((NSAMP, POOL_BUF, 4, NSAMP), np.float32)
    for g, w in enumerate(WINDOWS):
        rcnt[:, g] = 1.0 / np.minimum(np.arange(16) + 1, w)
        for b in range(NSAMP):
            win[b, POOL_BUF - (w - 1):, g, b] = 1.0
    return {"c_ident": np.eye(P, dtype=np.float32), "c_masks": masks, "c_rcnt": rcnt,
            "c_win": win.reshape(NSAMP * POOL_BUF, 4, NSAMP)}


def kernel(**inputs):
    import concourse.bacc as _bacc
    from concourse.bass_utils import run_bass_kernel_spmd as _run

    nc = _bacc.Bacc("TRN2", target_bir_lowering=False, num_devices=1)
    arrays, io = {}, {}
    given = {n: np.ascontiguousarray(inputs[n]) for n in _INS} | _constants()
    for name, a in given.items():
        arrays[f"in_{name}_dram"] = a
        io[name] = nc.dram_tensor(f"in_{name}_dram", a.shape, mybir.dt.from_np(a.dtype), kind="ExternalInput").ap()
    for name, shape in _OUTS:
        io[name] = nc.dram_tensor(f"out_{name}_dram", shape, F32, kind="ExternalOutput").ap()
    build(nc, io)
    r = _run(nc, [arrays], core_ids=[0])
    return tuple(r.results[0][f"out_{name}_dram"] for name, _ in _OUTS)
```

```python
from contextlib import ExitStack

import numpy as np

import concourse.bass as bass
from concourse import mybir

ALU = mybir.AluOpType
ACT = mybir.ActivationFunctionType
F32 = mybir.dt.float32
F16 = mybir.dt.float16
U8 = mybir.dt.uint8

P = 128
D = 2048
KT = D // P
SEQ = 256
NSAMP = 8
TOK = SEQ + NSAMP
HEADS = 8
DK = 128
PAIRS = HEADS // 2
WINDOWS = (2, 4, 8, 16)
POOL_BUF = max(WINDOWS) - 1
PLE = 256
DFF = 5632
FT = DFF // P
EPS = 1e-6
LEVELS = 8

COLS = 512
BLOCK_KT = 2
TPG = COLS // P
RAW_SLOTS = 4
HL_SLOTS = 8
AHEAD = 4

WSCALE = 1024.0
NSCALE = 8.0
HSCALE = 0.25
C_N = 1.0 / (WSCALE * NSCALE)
C_FFN = C_N
C_FF = 1.0 / WSCALE
C_H = 1.0 / (WSCALE * HSCALE)
QSCALE = DK ** -0.5

VEC_ROWS = (("g_mix", KT), ("g_ffn", KT), ("g_ple", KT), ("g_final", KT),
            ("pool_scale", 8), ("lb_logits", 8), ("g_head", 1))
VEC_AT = {}
for _name, _n in VEC_ROWS:
    VEC_AT[_name] = (sum(n for _, n in VEC_ROWS[:len(VEC_AT)]), _n)
NVEC = sum(n for _, n in VEC_ROWS)


class Stage:

    def __init__(self, prev, groups, bpg, closed=False, vstep=None, after_pad=False, dmas=1):
        self.dmas = dmas
        self.groups, self.bpg, self.closed, self.after_pad = groups, bpg, closed, after_pad
        self.vstep = vstep or bpg
        self.b0 = prev.b_end if prev else 0
        self.v0 = prev.v_end if prev else 0
        self.t0 = prev.t_end if prev else 0
        self.a0 = prev.a_end if prev else 0
        self.l0 = list(prev.l_end) if prev else [0] * RAW_SLOTS
        self.b_end = self.b0 + groups * bpg
        self.v_end = self.v0 + groups * self.vstep
        closings = groups * (bpg if closed else 1)
        self.t_end = self.t0 + TPG * closings
        self.a_end = self.a0 + (TPG - 1) * closings
        self.per = [sum((self.v0 + j) % RAW_SLOTS == s for j in range(bpg)) for s in range(RAW_SLOTS)]
        self.l_end = [self.l0[s] + groups * self.per[s] * dmas for s in range(RAW_SLOTS)]

    def block(self, i, j):
        return i * self.bpg + (self.b0 + j)

    def raw_slot(self, j):
        return (self.v0 + j) % RAW_SLOTS

    def hl_slot(self, j):
        return (self.v0 + j) % HL_SLOTS

    def landed(self, i, j):
        s = self.raw_slot(j)
        own = sum(self.raw_slot(k) == s for k in range(j + 1))
        return i * (self.per[s] * self.dmas) + (self.l0[s] + own * self.dmas)

    def padded(self, i):
        return self.vstep != self.bpg or (self.after_pad and isinstance(i, int) and i == 0)

    def raw_before(self, i, j):
        return 2 if self.padded(i) and j < 2 else RAW_SLOTS

    def hl_before(self, i, j):
        return 6 if self.padded(i) and j < 6 else HL_SLOTS

    def tile(self, i, n, j=0):
        return (j * TPG if self.closed else i * TPG) + (self.t0 + n)

    def tile_done(self, i, n, j=0):
        if n == TPG - 1:
            return "used", self.block(i, j if self.closed else self.bpg - 1) + 1
        return "acc_done", (j if self.closed else i) * (TPG - 1) + (self.a0 + n + 1)


S_IN = Stage(None, 10, 8)
S_POOL = Stage(S_IN, 1, 2, closed=True)
S_OUT = Stage(S_POOL, 4, 8)
S_PLE = Stage(S_OUT, 1, 4, closed=True)
S_FFN = Stage(S_PLE, DFF // 256, 8, dmas=2)
S_DOWN = Stage(S_FFN, 4, FT // BLOCK_KT, vstep=24)
S_GATE = Stage(S_DOWN, 4, 8, after_pad=True)
NBLOCKS = S_GATE.b_end
SIG_FFN = 6 * TPG
SIG_GATE = SIG_FFN + 2 * S_FFN.groups
G_MAIN = 6
G_COLS = (8, 9, 6, 7)

JOBS = [("vec", "dve")]
JOBS += [(f"n1_{k}", "dve") for k in range(KT)]
JOBS += [(f"pt_{k}", "dve") for k in range(2)]
JOBS += [("sb", "dve")]
for _p in range(PAIRS):
    JOBS += [(f"kv_{_p}", "dve"), (f"vt_{_p}", "act")]
    JOBS += [(f"lv_{_p}_{l}", "dve") for l in range(3)]
    JOBS += [(f"ou_{2 * _p}_0", "dve"), (f"ou_{2 * _p}_1", "dve")]
    JOBS += [(f"lv_{_p}_{l}", "dve") for l in range(3, LEVELS)]
    JOBS += [(f"cr_{_p}", "act"), (f"ks_{_p}", "act")]
    JOBS += [(f"ou_{2 * _p + 1}_0", "dve"), (f"ou_{2 * _p + 1}_1", "dve")]
    JOBS += [(f"o_{_p}", "act"), (f"sf_{_p}", "act"), (f"os_{_p}", "dve")]
    if _p == 1:
        JOBS += [("ut_0", "act"), ("ut_1", "act")]
JOBS += [(f"xt_{k}", "act") for k in range(KT // 2)]
JOBS += [("oss", "dve")]
JOBS += [(f"ot_{j}", "dve") for j in range(PAIRS)]
JOBS += [(f"xt_{k}", "act") for k in range(KT // 2, KT)]
JOBS += [("hs", "dve"), ("es", "dve")]
Y_EARLY = KT - TPG
JOBS += [(f"yt_{k}", "act" if k % 2 else "dve") for k in range(Y_EARLY)]
JOBS += [("ys", "dve")] + [(f"yt_{k}", "act" if k % 2 else "dve") for k in range(Y_EARLY, KT)]
JOB = {name: n for n, (name, _) in enumerate(JOBS)}
JOB_BANKS = 4
MASKS = P + (LEVELS - 1) * (P // 2)


def job_value(name):
    return JOB[name] + 1


def drained_value(n):
    return sum(e == JOBS[n][1] for _, e in JOBS[:n + 1])


def drain_of(name):
    return JOBS[JOB[name]][1], drained_value(JOB[name])


def build(nc, io):
    with ExitStack() as ctx:
        def sb(name, shape, dt=F32):
            return ctx.enter_context(nc.sbuf_tensor(name, shape, dt))

        def sem(name):
            return ctx.enter_context(nc.semaphore(name))

        raw = sb("raw", [P, RAW_SLOTS, BLOCK_KT * COLS])
        hi = sb("hi", [P, HL_SLOTS, BLOCK_KT * COLS], F16)
        lo = sb("lo", [P, HL_SLOTS, BLOCK_KT * COLS], F16)
        nrm = sb("nrm", [P, KT * TOK])
        mix = sb("mix", [P, KT * TOK])
        xe = sb("xe", [P, 3 * D])
        big = sb("big", [P, 6 * HEADS * TOK])
        hid = sb("hid", [P, KT * TOK])

        n_hi = nrm[:, 0:KT * TOK // 2].bitcast(F16).rearrange("p (k t) -> p k t", t=TOK)
        n_lo = nrm[:, KT * TOK // 2:].bitcast(F16).rearrange("p (k t) -> p k t", t=TOK)
        m_hi = mix[:, 0:KT * TOK // 2].bitcast(F16).rearrange("p (k t) -> p k t", t=TOK)
        m_lo = mix[:, KT * TOK // 2:].bitcast(F16).rearrange("p (k t) -> p k t", t=TOK)
        x_tok = xe[:, 0:2 * D].rearrange("p (a d) -> p a d", a=2)
        x_smp = xe[0:NSAMP, 2 * D:3 * D]
        e_all = xe[:, 0:KT * TOK].rearrange("p (k t) -> p k t", t=TOK)
        h_all = hid[:, :].rearrange("p (k t) -> p k t", t=TOK)

        def part(n):
            return big[:, n * HEADS * TOK:(n + 1) * HEADS * TOK].rearrange("p (h t) -> p h t", t=TOK)

        q_all, f_all, k_all, v_all, sg_all, u_all = (part(n) for n in range(6))
        pd_all = u_all
        FFW = FT * TOK // 2
        ff_hi = big[:, 0:FFW].bitcast(F16).rearrange("p (k t) -> p k t", t=TOK)
        ff_lo = big[:, FFW:2 * FFW].bitcast(F16).rearrange("p (k t) -> p k t", t=TOK)
        xn_tok = big[:, 0:2 * D].rearrange("p (a d) -> p a d", a=2)
        xn_smp = big[0:NSAMP, 2 * D:3 * D]
        ple_tok = big[:, 3 * D:3 * D + 2 * PLE].rearrange("p (a d) -> p a d", a=2)
        ple_smp = big[0:NSAMP, 3 * D + 2 * PLE:3 * D + 3 * PLE]
        vec_rows = big[0:NVEC, 3 * D + 3 * PLE:3 * D + 3 * PLE + P]
        junk = big[:, 4 * D:5 * D]
        masks_f = big[:, 5 * D:5 * D + MASKS]
        e_sq = mix[:, :]
        y_tok = big[:, 0:2 * D].rearrange("p (a d) -> p a d", a=2)
        y_smp = big[0:NSAMP, 2 * D:3 * D]
        pd_hi = nrm[:, 0:HEADS * TOK // 2].bitcast(F16).rearrange("p (k t) -> p k t", t=TOK)
        pd_lo = nrm[:, HEADS * TOK // 2:HEADS * TOK].bitcast(F16).rearrange("p (k t) -> p k t", t=TOK)
        lev = mix[:, 0:LEVELS * 2 * SEQ].rearrange("p (l h t) -> p l h t", l=LEVELS, h=2)
        pre = hid[:, 0:512].rearrange("p (h t) -> p h t", h=2)
        suf = hid[:, 512:1024].rearrange("p (h t) -> p h t", h=2)
        k_end = hid[:, 1024:1536].rearrange("p (h t) -> p h t", h=2)
        k_end_tok = hid[:, 512:1024].rearrange("p (h a d) -> p h a d", h=2, a=2)
        v_tok = hid[:, 1536:2048].rearrange("p (h a v) -> p h a v", h=2, a=2)
        buf_tok = hid[0:NSAMP * POOL_BUF, 2048:3072]
        win = [hid[:, 2048 + 512 * n:2560 + 512 * n].rearrange("p (h t) -> p h t", h=2) for n in range(2)]
        k_mask = hid[0:4 * NSAMP, 3072:3584].bitcast(F16).rearrange("p (b d) -> p b d", b=NSAMP)

        scores = sb("scores", [P, 3, 2, P])
        k4 = sb("k4", [P, HEADS, 4, NSAMP], F16)
        v4 = sb("v4", [P, HEADS, 4, NSAMP], F16)
        kv_smp = sb("kv_smp", [4 * NSAMP, 4, P], F16)
        sb_sum = sb("sb_sum", [P, 8, NSAMP])
        state = sb("state", [P, 2, NSAMP, P])
        s_final = sb("s_final", [P, 2, P])
        o_tok = sb("o_tok", [P, HEADS, 2, P])
        gate_t = sb("gate_t", [P, TPG, TOK])
        a32 = sb("a32", [P, 2, TOK])
        tg32 = sb("tg32", [P, 2, TOK])
        ident = sb("ident", [P, P])
        ones = sb("ones", [P, P])
        ident16 = sb("ident16", [P, P], F16)
        delta = sb("delta", [4 * NSAMP, NSAMP])
        masks = sb("masks", [P, MASKS], U8)
        rcnt = sb("rcnt", [P, 4, 16])
        win_sel = sb("win_sel", [NSAMP * POOL_BUF, 4, NSAMP])
        vec = sb("vec", [P, NVEC])
        gm8 = sb("gm8", [P, KT])
        gf8 = sb("gf8", [P, KT])
        gh8 = sb("gh8", [P, 1])
        ps8 = sb("ps8", [P, 8])
        lbt = sb("lbt", [P, 4, 8])
        nomlb = sb("nomlb", [P, 8])
        ss = sb("ss", [P, 3])
        rs = sb("rs", [P, 3])
        rt = sb("rt", [P, HEADS * 2])
        ss_o = sb("ss_o", [P, HEADS, 2])
        rs_o = sb("rs_o", [P, HEADS, 2])
        o_smp = sb("o_smp", [P, HEADS, NSAMP])
        o_sq = sb("o_sq", [P, HEADS, NSAMP])
        o_ms = sb("o_ms", [P, HEADS, NSAMP])
        pt_hi = sb("pt_hi", [P, 2, TOK], F16)
        pt_lo = sb("pt_lo", [P, 2, TOK], F16)
        u_last = o_tok[0:POOL_BUF + NSAMP, 4:8].rearrange("p h a v -> p (h a v)")
        h_sq, h_ssq = a32[:, 0, :], a32[:, 1, :]
        rstd_bc = gate_t[:, TPG - 1, :]

        acc = ctx.enter_context(nc.psum_tensor("acc", [P, TPG, 512], F32))
        wrk = ctx.enter_context(nc.psum_tensor("wrk", [P, JOB_BANKS, 512], F32))

        landed = [sem(f"landed{s}") for s in range(RAW_SLOTS)]
        hi_done, lo_done, used = sem("hi_done"), sem("lo_done"), sem("used")
        acc_done, acc_free = sem("acc_done"), sem("acc_free")
        gate_ready = sem("gate_ready")
        job_done = sem("job_done")
        drained = {"act": sem("drained_act"), "dve": sem("drained_dve")}
        x_in = [sem("x_in0"), sem("x_in1"), sem("x_in_smp")]
        id_in, c_in, v_in, p_in, buf_in = sem("id_in"), sem("c_in"), sem("v_in"), sem("p_in"), sem("buf_in")
        state_in = [sem("state_in0"), sem("state_in1")]
        state_out = [sem("state_out0"), sem("state_out1")]
        stored, buf_stored = sem("stored"), sem("buf_stored")
        const_ready = sem("const_ready")
        sq_ready, mean_ready, rstd_ready, xn_ready = sem("sq_ready"), sem("mean_ready"), sem("rstd_ready"), sem("xn_ready")
        n_hi_ready, n_ready = sem("n_hi_ready"), sem("n_ready")
        lev_ready, zero_ready, kmask_ready = sem("lev_ready"), sem("zero_ready"), sem("kmask_ready")
        sf_out = sem("sf_out")
        pool_ready, pd_hi_ready, pd_ready = sem("pool_ready"), sem("pd_hi_ready"), sem("pd_ready")
        mix_tmp, mix_hi, mix_ready = sem("mix_tmp"), sem("mix_hi"), sem("mix_ready")
        chain = sem("chain")
        pool_chain = sem("pool_chain")
        esum_ready = sem("esum_ready")
        out_chain, ffn_chain, down_chain, gate_chain = (sem(n) for n in ("out_chain", "ffn_chain", "down_chain", "gate_chain"))
        e_rstd, e_ready, osq_ready, kv4_ready, xn_bc, rs_final = sem("e_rstd"), sem("e_ready"), sem("osq_ready"), sem("kv4_ready"), sem("xn_bc"), sem("rs_final")
        y_scaled = sem("y_scaled")
        rs0_ready, xn_act = sem("rs0_ready"), sem("xn_act")
        ff_ready, hg_ready, xn_o = sem("ff_ready"), sem("hg_ready"), sem("xn_o")
        named = {"used": used, "acc_done": acc_done}

        def ntmp(k):
            return (a32, tg32)[k % 4 // 2][:, k % 2, :]

        def y_out(eng, k, scaled):
            name = f"yt_{k}"
            eng.wait_ge(job_done, job_value(name))
            ps, cols = wrk[:, JOB[name] % JOB_BANKS, :], slice(k * P, (k + 1) * P)
            for a in range(2):
                scaled(y_tok[:, a, cols], ps[:, a * P:(a + 1) * P], rs[:, a:a + 1] if k >= Y_EARLY else 1.0)
            scaled(y_smp[:, cols], ps[0:NSAMP, SEQ:SEQ + P], rs[0:NSAMP, 2:3] if k >= Y_EARLY else 1.0).then_inc(drained[JOBS[JOB[name]][1]], 1)

        def wait_tile(eng, st, i, n, j=0):
            name, value = st.tile_done(i, n, j)
            eng.wait_ge(named[name], value)

        def rows(ap):
            return ap.rearrange("o (k p) n -> p (o k) n", p=P)

        w_in, w_out, w_ple, w_down, w_gate = (rows(io[n]) for n in ("w_in", "w_out", "w_ple", "w_down", "w_ple_gate"))
        w_gu = io["w_gate_up"].rearrange("o (k p) (s n) -> p (o k) s n", p=P, s=2)
        w_pool = io["w_pool"].rearrange("o g (k p) n -> p (o g) k n", p=P)

        block = ctx.enter_context(nc.Block())

        @block.sync
        def _(sp):
            def load(st, i, j, src, first=False):
                if not first:
                    sp.wait_ge(lo_done, st.block(i, j) - st.raw_before(i, j) + 1)
                s = st.raw_slot(j)
                dst = raw[:, s, :]
                if st.dmas == 2:
                    dst = dst.rearrange("p (k s n) -> p k s n", k=BLOCK_KT, s=2)
                    for half in range(2):
                        sp.dma_start(dst[:, :, half, :], src[:, :, half, :]).then_inc(landed[s], 16)
                    return
                if len(src.shape) == 3:
                    dst = dst.rearrange("p (k n) -> p k n", k=src.shape[1])
                elif len(src.shape) == 4:
                    dst = dst.rearrange("p (g k n) -> p g k n", g=src.shape[1], k=src.shape[2])
                sp.dma_start(dst, src).then_inc(landed[s], 16)

            def std(w):
                return lambda i, j: w[:, 2 * j:2 * j + 2, bass.ds(i * COLS, COLS)]

            def out_block(j):
                return (j + 4) % 8

            def gate_up(i, j):
                return w_gu[:, 2 * j:2 * j + 2, :, bass.ds(i * 256, 256)]

            sp.dma_start(x_tok[:, 0, :], io["x_prompt"][0, 0:P, :]).then_inc(x_in[0], 16)
            sp.dma_start(x_tok[:, 1, :], io["x_prompt"][0, P:SEQ, :]).then_inc(x_in[1], 16)
            for j in range(8):
                load(S_IN, 0, j, std(w_in)(0, j), first=j < RAW_SLOTS)
            with sp.Fori(1, G_MAIN) as i:
                for j in range(8):
                    load(S_IN, i, j, std(w_in)(i, j))
            for i in range(G_MAIN, S_IN.groups):
                for j in range(8):
                    load(S_IN, i, j, std(w_in)(G_COLS[i - G_MAIN], j))
            for j in range(2):
                load(S_POOL, 0, j, w_pool[:, 2 * j:2 * j + 2, :, :])
            for i in range(S_OUT.groups):
                for j in range(8):
                    load(S_OUT, i, j, std(w_out)(i, out_block(j)))
            for j in range(4):
                load(S_PLE, 0, j, w_ple[:, :, j * COLS:(j + 1) * COLS])
            with sp.Fori(0, S_FFN.groups) as i:
                for j in range(8):
                    load(S_FFN, i, j, gate_up(i, j))
            with sp.Fori(0, S_DOWN.groups) as i:
                for j in range(S_DOWN.bpg):
                    load(S_DOWN, i, j, std(w_down)(i, j))
            for j in range(8):
                load(S_GATE, 0, j, std(w_gate)(0, j))
            with sp.Fori(1, S_GATE.groups) as i:
                for j in range(8):
                    load(S_GATE, i, j, std(w_gate)(i, j))
            for c in range(2):
                if c == 0:
                    sp.wait_ge(y_scaled, 3)
                else:
                    sp.wait_ge(drained["dve"], drain_of(f"yt_{KT - 2}")[1])
                    sp.wait_ge(drained["act"], drain_of(f"yt_{KT - 1}")[1])
                cols = (slice(0, Y_EARLY * P), slice(Y_EARLY * P, D))[c]
                sp.dma_start(io["y_prompt"][0, :, cols].rearrange("(a p) d -> p a d", p=P), y_tok[:, :, cols])\
                    .then_inc(stored, 16)
                sp.dma_start(io["y_sample"][:, 0, cols], y_smp[:, cols]).then_inc(stored, 16)
            sp.wait_ge(stored, 16 * 4)
            sp.wait_ge(buf_stored, 16 * 3)
            sp.wait_ge(sf_out, 16 * PAIRS)
            sp.wait_ge(state_out[0], 16 * PAIRS)
            sp.wait_ge(state_out[1], 16 * PAIRS)

        @block.gpsimd
        def _(pool):
            links = [0]

            def link(ins):
                links[0] += 1
                ins.then_inc(pool_chain, 1)
                pool.wait_ge(pool_chain, links[0])

            def load_state(h):
                pool.dma_start(state[:, h % 2, :, :], io["state_hgrn"][0, :, h, :, :].rearrange("b d v -> d b v"))\
                    .then_inc(state_in[h % 2], 16)

            for name, n in VEC_ROWS:
                at = VEC_AT[name][0]
                src = io[name].rearrange("a (k p) -> (a k) p", p=P) if name != "g_final" else \
                    io[name].rearrange("(k p) -> k p", p=P)
                pool.dma_start(vec_rows[at:at + n, :], src).then_inc(v_in, 16)
            pool.dma_start(masks_f, io["c_masks"]).then_inc(c_in, 16)
            pool.dma_start(rcnt[:], io["c_rcnt"]).then_inc(c_in, 16)
            pool.dma_start(win_sel[:], io["c_win"]).then_inc(c_in, 16)
            pool.dma_start(delta[:], io["c_delta"]).then_inc(c_in, 16)
            pool.dma_start(ple_tok, io["p_prompt"][0, 0].rearrange("(a p) d -> p a d", p=P)).then_inc(p_in, 16)
            pool.dma_start(ple_smp, io["p_sample"][0, :, 0, :]).then_inc(p_in, 16)
            pool.wait_ge(lo_done, 8)
            load_state(0)
            load_state(1)
            pool.dma_start(buf_tok, io["state_pool"][0].rearrange("b j c -> (b j) c")).then_inc(buf_in, 16)
            pool.dma_start(io["new_pool_sample"][0, :, 0:POOL_BUF - 1, :], io["state_pool"][0, :, 1:POOL_BUF, :])\
                .then_inc(buf_stored, 16)
            def windows(gs):
                for g in gs:
                    w = WINDOWS[g]
                    u = u_all[:, 2 * g:2 * g + 2, 0:SEQ]
                    src, m, n = u, 1, 0
                    while m < w:
                        dst = win[n % 2]
                        nc.gpsimd.tensor_copy(dst[:, :, 0:m], src[:, :, 0:m])
                        link(nc.gpsimd.tensor_tensor(dst[:, :, m:SEQ], src[:, :, m:SEQ], src[:, :, 0:SEQ - m], ALU.add))
                        src, m, n = dst, 2 * m, n + 1
                    nc.gpsimd.tensor_tensor(src[:, :, 0:16], src[:, :, 0:16],
                                            rcnt[:, g, :].unsqueeze(1).to_broadcast([P, 2, 16]), ALU.mult)
                    link(nc.gpsimd.tensor_scalar(src[:, :, 16:SEQ], src[:, :, 16:SEQ], 1.0 / w, None, ALU.mult))
                    nc.gpsimd.tensor_tensor(u, src, u, ALU.subtract).then_inc(pool_ready, 1)
                    pool.wait_ge(pool_ready, g + 1)

            nc.gpsimd.memset(scores[:, 0:2], 0.0).then_inc(zero_ready, 1)
            for p in range(PAIRS):
                if p == 2:
                    pool.wait_ge(drained["act"], drain_of("ut_1")[1])
                    pool.dma_start(io["new_pool_prompt"][0, 0, :, :], u_last[0:POOL_BUF, :]).then_inc(buf_stored, 16)
                    pool.dma_start(io["new_pool_sample"][0, :, POOL_BUF - 1, :], u_last[POOL_BUF:, :]).then_inc(buf_stored, 16)
                for h in (2 * p, 2 * p + 1):
                    if h % 2 == 0:
                        pool.wait_ge(drained["dve"], drain_of(f"kv_{p}")[1])
                        pool.wait_ge(c_in, 16 * 4)
                    if h:
                        pool.wait_ge(job_done, job_value(f"ou_{h - 1}_1"))
                    nc.gpsimd.tensor_tensor(
                        k_mask, kv_smp[:, h % 2, :].unsqueeze(1).to_broadcast([4 * NSAMP, NSAMP, P]),
                        delta[:].unsqueeze(2).to_broadcast([4 * NSAMP, NSAMP, P]),
                        ALU.mult).then_inc(kmask_ready, 1)
                    if p >= 2 and h % 2 == 0:
                        pool.wait_ge(job_done, job_value("ut_1"))
                        windows((0, 1) if p == 2 else (2, 3))
                for h in (2 * p, 2 * p + 1):
                    pool.wait_ge(drained["dve"], drain_of(f"ou_{h}_1")[1])
                    pool.dma_start(io["new_hgrn_sample"][0, :, h, :, :].rearrange("b d v -> d b v"),
                                   state[:, h % 2, :, :]).then_inc(state_out[h % 2], 16)
                if p + 1 < PAIRS:
                    pool.wait_ge(job_done, job_value(f"o_{p}"))
                    nc.gpsimd.memset(scores[:, 0:2], 0.0).then_inc(zero_ready, 1)
                    pool.wait_ge(job_done, job_value(f"os_{p}"))
                    for h in (2 * p + 2, 2 * p + 3):
                        pool.wait_ge(state_out[h % 2], 16 * (p + 1))
                        load_state(h)
            pool.wait_ge(xn_bc, 1)
            for k in range(KT):
                if k >= 4:
                    pool.wait_ge(n_ready, k - 3)
                nc.gpsimd.tensor_tensor(ntmp(k), h_all[:, k, :], rstd_bc, ALU.mult).then_inc(xn_ready, 1)
            pool.wait_ge(acc_free, S_PLE.t_end)
            link(nc.gpsimd.tensor_tensor(e_sq, xe[:, 0:KT * TOK], xe[:, 0:KT * TOK], ALU.mult))
            n = KT // 2
            while n:
                step = nc.gpsimd.tensor_tensor(e_sq[:, 0:n * TOK], e_sq[:, 0:n * TOK], e_sq[:, n * TOK:2 * n * TOK], ALU.add)
                if n > 1:
                    link(step)
                else:
                    step.then_inc(esum_ready, 1)
                n //= 2
            pool.wait_ge(e_rstd, 1)
            for k in range(KT):
                last = nc.gpsimd.tensor_tensor(e_all[:, k, :], e_all[:, k, :], rstd_bc, ALU.mult)
            last.then_inc(e_ready, 1)

        @block.scalar
        def _(act):
            def split(st, i, j):
                act.wait_ge(landed[st.raw_slot(j)], 16 * st.landed(i, j))
                b = st.block(i, j)
                if not (isinstance(b, int) and b < HL_SLOTS):
                    act.wait_ge(used, b - st.hl_before(i, j) + 1)
                nc.scalar.activation(hi[:, st.hl_slot(j), :], raw[:, st.raw_slot(j), :], ACT.Copy,
                                     scale=WSCALE).then_inc(hi_done, 1)

            def gates(st, i, ns, c, j=0, reuse=False):
                for n in ns:
                    if reuse:
                        act.wait_ge(acc_free, st.tile(i, n) - (TPG - 1))
                    wait_tile(act, st, i, n, j)
                    nc.scalar.activation(gate_t[:, n, :], acc[:, n, 0:TOK], ACT.Sigmoid, scale=c).then_inc(gate_ready, 1)

            def group(st, i, evac, nxt=None, between=None):
                for j in range(AHEAD, st.bpg):
                    split(st, i, j)
                    if between and j == AHEAD + 1:
                        between()
                if nxt is None:
                    for j in range(AHEAD):
                        split(st, i + 1, j)
                else:
                    for j in range(min(AHEAD, nxt.bpg)):
                        split(nxt, 0, j)
                evac()

            def wait_job(name):
                act.wait_ge(job_done, job_value(name))

            act.dma_start(x_smp, io["x_sample"][:, 0, :]).then_inc(x_in[2], 16)
            act.dma_start(ident[:], io["c_ident"]).then_inc(id_in, 16)
            act.wait_ge(const_ready, 1)
            for n, a in enumerate((2, 0, 1)):
                act.wait_ge(x_in[a], 16)
                if n:
                    act.wait_ge(sq_ready, n)
                m, src = (NSAMP, x_smp) if a == 2 else (P, x_tok[:, a, :])
                nc.scalar.activation(junk[0:m, :], src, ACT.Square, accum_out=ss[0:m, a:a + 1]).then_inc(sq_ready, 1)
            act.wait_ge(mean_ready, 1)
            nc.scalar.activation(rs[:], rs[:], ACT.Sqrt).then_inc(rstd_ready, 1)
            act.wait_ge(rs0_ready, 1)
            nc.scalar.activation(xn_tok[:, 1, :], x_tok[:, 1, :], ACT.Copy, scale=rs[:, 1:2]).then_inc(xn_act, 1)
            split(S_IN, 0, 0)
            act.wait_ge(const_ready, 2)
            for k in range(KT):
                if k % 4 == 2 and k > 4:
                    split(S_IN, 0, k // 4)
                wait_job(f"n1_{k}")
                nc.scalar.activation(n_hi[:, k, :], wrk[:, JOB[f"n1_{k}"] % JOB_BANKS, 0:TOK], ACT.Copy,
                                     scale=gm8[:, k:k + 1]).then_inc(n_hi_ready, 1)
            nc.scalar.activation(lbt[:, 1, :], lbt[:, 0, :], ACT.Exp).then_inc(rstd_ready, 1)
            group(S_IN, 0, lambda: gates(S_IN, 0, range(TPG), C_N))
            with act.Fori(1, 4) as i:
                group(S_IN, i, lambda: gates(S_IN, i, range(TPG), C_N))
            with act.Fori(4, G_MAIN) as i:
                group(S_IN, i, lambda: None)
            for p in range(PAIRS):
                i = G_MAIN + p

                def take_v():
                    wait_job(f"vt_{p}")
                    nc.scalar.activation(v_tok, wrk[:, JOB[f"vt_{p}"] % JOB_BANKS, :].rearrange("p (h a v) -> p h a v", h=2, a=2),
                                         ACT.Copy).then_inc(drained["act"], 1)

                group(S_IN, i, (lambda: gates(S_IN, i, range(TPG), C_N)) if i >= 8 else (lambda: None),
                      S_POOL if i == 9 else None, take_v)
                wait_job(f"cr_{p}")
                nc.scalar.activation(scores[:, 2], wrk[:, JOB[f"cr_{p}"] % JOB_BANKS, 0:256].rearrange("p (h t) -> p h t", h=2),
                                     ACT.Copy).then_inc(drained["act"], 1)
                if p == PAIRS - 1:
                    act.wait_ge(pool_ready, len(WINDOWS))
                    act.wait_ge(pd_ready, 1)
                    act.wait_ge(used, S_IN.b_end)
                    nc.scalar.activation(pd_hi, pd_all, ACT.Copy, scale=NSCALE).then_inc(pd_hi_ready, 1)
                wait_job(f"ks_{p}")
                nc.scalar.activation(k_end_tok, wrk[:, JOB[f"ks_{p}"] % JOB_BANKS, :].rearrange("p (h a v) -> p h a v", h=2, a=2),
                                     ACT.Copy).then_inc(drained["act"], 1)
                wait_job(f"o_{p}")
                o_ps = wrk[:, JOB[f"o_{p}"] % JOB_BANKS, :].rearrange("p (h a v) -> p h a v", h=2, a=2)
                for h in range(2):
                    for a in range(2):
                        nc.scalar.activation(gate_t[:, 2 * h + a, 0:P], o_ps[:, h, a, :], ACT.Square,
                                             accum_out=ss_o[:, 2 * p + h, a:a + 1])
                if p == 2:
                    act.wait_ge(buf_stored, 16 * 3)
                nc.scalar.activation(o_tok[:, 2 * p:2 * p + 2], o_ps, ACT.Copy).then_inc(drained["act"], 1)
                wait_job(f"sf_{p}")
                if p:
                    act.wait_ge(sf_out, 16 * p)
                nc.scalar.activation(s_final[:], wrk[:, JOB[f"sf_{p}"] % JOB_BANKS, 0:256].rearrange("p (h v) -> p h v", h=2),
                                     ACT.Copy).then_inc(drained["act"], 1)
                act.wait_ge(drained["act"], drain_of(f"sf_{p}")[1])
                act.dma_start(io["new_hgrn_prompt"][0, 0, 2 * p:2 * p + 2].rearrange("h d v -> d h v"), s_final[:])\
                    .then_inc(sf_out, 16)
                if p == 1:
                    for n in range(2):
                        wait_job(f"ut_{n}")
                        nc.scalar.activation(u_last[:, n * 512:(n + 1) * 512],
                                             wrk[0:POOL_BUF + NSAMP, JOB[f"ut_{n}"] % JOB_BANKS, :], ACT.Copy)\
                            .then_inc(drained["act"], 1)
            act.wait_ge(mean_ready, 2)
            nc.scalar.activation(rs_o[:], rs_o[:], ACT.Sqrt).then_inc(rstd_ready, 1)
            for j in range(2):
                for b in (2 * j, 2 * j + 1):
                    split(S_OUT, 0, b)
                for n in range(TPG):
                    wait_tile(act, S_POOL, 0, n, j)
                    k = TPG * j + n
                    nc.scalar.activation(m_hi[:, 8 + k, :], acc[:, n, 0:TOK], ACT.Copy, scale=ps8[:, k:k + 1])\
                        .then_inc(mix_hi, 1)
            def x_tile(k):
                wait_job(f"xt_{k}")
                nc.scalar.activation(h_all[:, k, :], wrk[:, JOB[f"xt_{k}"] % JOB_BANKS, 0:TOK], ACT.Copy)\
                    .then_inc(drained["act"], 1)

            for k in range(KT // 2):
                x_tile(k)
            act.wait_ge(mean_ready, 3)
            nc.scalar.activation(o_sq[:], o_sq[:], ACT.Sqrt).then_inc(rstd_ready, 1)
            for j in range(PAIRS):
                act.wait_ge(mix_tmp, j + 1)
                nc.scalar.activation(m_hi[:, 2 * j:2 * j + 2, 0:SEQ], (a32, tg32)[j % 2][:, :, 0:SEQ], ACT.Copy)\
                    .then_inc(mix_hi, 1)
            for k in range(KT // 2, KT):
                x_tile(k)
            with act.Fori(0, S_OUT.groups - 1) as i:
                group(S_OUT, i, lambda: None)
            group(S_OUT, S_OUT.groups - 1, lambda: None, S_PLE)
            act.wait_ge(acc_free, S_PLE.t0)
            for j in range(4):
                split(S_FFN, 0, j)
                for n in range(TPG):
                    wait_tile(act, S_PLE, 0, n, j)
                    nc.scalar.activation(e_all[:, TPG * j + n, :], acc[:, n, 0:TOK], ACT.Copy, scale=C_N)\
                        .then_inc(acc_free, 1)
                if j == 1:
                    act.wait_ge(mean_ready, 4)
                    nc.scalar.activation(rstd_bc, rstd_bc, ACT.Sqrt).then_inc(rstd_ready, 1)
                for k in ((), (), range(0, 4), range(4, KT))[j]:
                    act.wait_ge(xn_ready, 2 + k + 1)
                    nc.scalar.activation(n_hi[:, k, :], ntmp(k), ACT.Copy, scale=gf8[:, k:k + 1]).then_inc(n_hi_ready, 1)
            with act.Fori(0, S_FFN.groups - 1) as i:
                group(S_FFN, i, lambda: gates(S_FFN, i, range(2), C_FFN))
            group(S_FFN, S_FFN.groups - 1, lambda: gates(S_FFN, S_FFN.groups - 1, range(2), C_FFN), S_DOWN)
            act.wait_ge(mean_ready, 5)
            nc.scalar.activation(rstd_bc, rstd_bc, ACT.Sqrt).then_inc(rstd_ready, 1)
            with act.Fori(0, S_DOWN.groups - 1) as i:
                group(S_DOWN, i, lambda: None)
            group(S_DOWN, S_DOWN.groups - 1, lambda: None, S_GATE)
            act.wait_ge(e_ready, 1)
            group(S_GATE, 0, lambda: gates(S_GATE, 0, range(TPG), C_H))
            with act.Fori(1, S_GATE.groups - 1) as i:
                group(S_GATE, i, lambda: gates(S_GATE, i, range(TPG), C_H, reuse=True))
            last = S_GATE.groups - 1
            for j in range(AHEAD, 8):
                split(S_GATE, last, j)

            def y_part(ks):
                for k in ks:
                    y_out(act, k, lambda out, src, scale: nc.scalar.activation(out, src, ACT.Copy, scale=scale))

            y_part(range(1, Y_EARLY, 2))
            gates(S_GATE, last, range(TPG), C_H, reuse=True)
            act.wait_ge(mean_ready, 6)
            nc.scalar.activation(rs[:], rs[:], ACT.Sqrt).then_inc(rstd_ready, 1)
            act.wait_ge(rs_final, 1)
            act.wait_ge(drained["dve"], drain_of(f"yt_{Y_EARLY - 2}")[1])
            act.wait_ge(drained["act"], drain_of(f"yt_{Y_EARLY - 1}")[1])
            nc.scalar.activation(y_tok[:, 1, 0:Y_EARLY * P], y_tok[:, 1, 0:Y_EARLY * P], ACT.Copy, scale=rs[:, 1:2])\
                .then_inc(y_scaled, 1)
            y_part(range(Y_EARLY + 1, KT, 2))

        @block.vector
        def _(dve):
            links = [0]
            stt, ts, tt = nc.vector.scalar_tensor_tensor, nc.vector.tensor_scalar, nc.vector.tensor_tensor

            def link(ins):
                if isinstance(ins, str):
                    dve.wait_ge(drained["dve"], drain_of(ins)[1])
                    return
                links[0] += 1
                ins.then_inc(chain, 1)
                dve.wait_ge(chain, links[0])

            def split(st, i, j):
                dve.wait_ge(hi_done, st.block(i, j) + 1)
                stt(lo[:, st.hl_slot(j), :], raw[:, st.raw_slot(j), :], WSCALE, hi[:, st.hl_slot(j), :],
                    ALU.mult, ALU.subtract).then_inc(lo_done, 1)

            def group(st, i, evac, nxt=None, between=None):
                later = [(st, i, j) for j in range(AHEAD, st.bpg)]
                later += [(st, i + 1, j) for j in range(AHEAD)] if nxt is None else \
                    [(nxt, 0, j) for j in range(min(AHEAD, nxt.bpg))]
                for n, s in enumerate(later):
                    split(*s)
                    if between:
                        between(n)
                evac()

            def wait_job(name):
                dve.wait_ge(job_done, job_value(name))

            def newton(r, v, tmp):
                link(stt(tmp, r, -0.5, r, ALU.mult, ALU.mult))
                link(tt(tmp, tmp, v, ALU.mult))
                return stt(r, tmp, 1.5, r, ALU.add, ALU.mult)

            def rstd_row(name, n):
                link(drain(ts(h_sq, bank(name)[:, 0:TOK], 1.0 / D, EPS, ALU.mult, ALU.add), name))
                nc.vector.reciprocal(rstd_bc, h_sq).then_inc(mean_ready, 1)
                dve.wait_ge(rstd_ready, n)
                return newton(rstd_bc, h_sq, tg32[:, 0, :])

            def drain(ins, name):
                ins.then_inc(drained["dve"], 1)
                return name

            def bank(name):
                return wrk[:, JOB[name] % JOB_BANKS, :]

            nc.vector.memset(ones[:], 1.0)
            nc.vector.memset(ss[:], 1.0).then_inc(const_ready, 1)
            dve.wait_ge(sq_ready, 3)
            link(ts(ss[:], ss[:], 1.0 / D, EPS, ALU.mult, ALU.add))
            nc.vector.reciprocal(rs[:], ss[:]).then_inc(mean_ready, 1)
            dve.wait_ge(rstd_ready, 1)
            newton(rs[:], ss[:], rt[:, 0:3]).then_inc(rs0_ready, 1)
            dve.wait_ge(rs0_ready, 1)
            dve.wait_ge(x_in[2], 16)
            dve.wait_ge(x_in[0], 16)
            ts(xn_smp, x_smp, rs[0:NSAMP, 2:3], None, ALU.mult).then_inc(xn_ready, 1)
            ts(xn_tok[:, 0, :], x_tok[:, 0, :], rs[:, 0:1], None, ALU.mult).then_inc(xn_ready, 1)
            wait_job("vec")
            drain(nc.vector.tensor_copy(vec[:], bank("vec")[:, 0:NVEC]), "vec")
            dve.wait_ge(drained["dve"], 1)

            def v(name):
                at, n = VEC_AT[name]
                return vec[:, at:at + n]

            ts(gf8[:], v("g_ffn"), NSCALE, None, ALU.mult)
            ts(gh8[:], v("g_head"), NSCALE, None, ALU.mult)
            ts(ps8[:], v("pool_scale"), NSCALE * C_N, None, ALU.mult)
            link(ts(gm8[:], v("g_mix"), NSCALE, None, ALU.mult))
            tt(lbt[:, 0, :], v("lb_logits"), v("lb_logits"), ALU.subtract).then_inc(const_ready, 1)
            dve.wait_ge(const_ready, 2)
            split(S_IN, 0, 0)
            for k in range(KT):
                if k % 4 == 2 and k > 4:
                    split(S_IN, 0, k // 4)
                dve.wait_ge(n_hi_ready, k + 1)
                drain(stt(n_lo[:, k, :], bank(f"n1_{k}")[:, 0:TOK], gm8[:, k:k + 1], n_hi[:, k, :],
                          ALU.mult, ALU.subtract), f"n1_{k}")
            dve.wait_ge(rstd_ready, 2)
            dve.wait_ge(c_in, 64)
            nc.vector.tensor_copy(ident16[:], ident[:])
            link(nc.vector.tensor_copy(masks[:], masks_f))
            link(nc.vector.reciprocal(lbt[:, 2, :], lbt[:, 1, :]))
            link(tt(lbt[:, 2, :], lbt[:, 1, :], lbt[:, 2, :], ALU.mult))
            link(tt(lbt[:, 0, :], lbt[:, 2, :], lbt[:, 2, :], ALU.subtract))
            link(ts(lbt[:, 3, :], lbt[:, 0, :], -1.0, 1.0, ALU.mult, ALU.add))
            ts(nomlb[:], lbt[:, 3, :], -1.0, None, ALU.mult)
            for k in range(2):
                wait_job(f"pt_{k}")
                link(ts(pt_hi[:, k, :], bank(f"pt_{k}")[:, 0:TOK], NSCALE, None, ALU.mult))
                drain(stt(pt_lo[:, k, :], bank(f"pt_{k}")[:, 0:TOK], NSCALE, pt_hi[:, k, :],
                          ALU.mult, ALU.subtract), f"pt_{k}")

            def one(x, i, n=0):
                return x[:, bass.ds(i * TPG + n, 1)]

            def tile_of(x, i, n):
                return one(x, i, n).rearrange("p a t -> p (a t)")

            def evac_q(i):
                for n in range(TPG):
                    dve.wait_ge(gate_ready, i * TPG + (n + 1))
                    stt(tile_of(q_all, i, n), acc[:, n, 0:TOK], C_N * QSCALE, gate_t[:, n, :],
                        ALU.mult, ALU.mult).then_inc(acc_free, 1)

            def evac_f(i):
                for n in range(TPG):
                    dve.wait_ge(gate_ready, i * TPG + (n + 1))
                    ts(tile_of(f_all, i - 2, n), gate_t[:, n, :], one(lbt[:, 3, :], i - 2, n),
                       one(lbt[:, 0, :], i - 2, n), ALU.mult, ALU.add)
                    ts(tile_of(k_all, i - 2, n), gate_t[:, n, :], one(nomlb, i - 2, n),
                       one(lbt[:, 3, :], i - 2, n), ALU.mult, ALU.add).then_inc(acc_free, 1)

            def evac_copy(dst, i, i0):
                for n in range(TPG):
                    wait_tile(dve, S_IN, i, n)
                    ts(tile_of(dst, i - i0, n), acc[:, n, 0:TOK], C_N, None, ALU.mult).then_inc(acc_free, 1)

            def evac_g(i):
                for n in range(TPG):
                    dve.wait_ge(gate_ready, 4 * TPG + (i - 8) * TPG + (n + 1))
                    stt(tile_of(sg_all, i - 8, n), acc[:, n, 0:TOK], C_N, gate_t[:, n, :],
                        ALU.mult, ALU.mult).then_inc(acc_free, 1)

            with dve.Fori(0, 2) as i:
                group(S_IN, i, lambda: evac_q(i))
            with dve.Fori(2, 4) as i:
                group(S_IN, i, lambda: evac_f(i))
            with dve.Fori(4, 6) as i:
                group(S_IN, i, lambda: evac_copy(v_all, i, 4))
            wait_job("sb")
            drain(nc.vector.tensor_copy(sb_sum[:].rearrange("p k b -> p (k b)"), bank("sb")[:, 0:64]), "sb")

            def halves(x, l):
                return x.rearrange("p h (n s k) -> p h n s k", s=2, k=1 << l)

            def level(p, l):
                hs = slice(2 * p, 2 * p + 2)
                q, k, f = (halves(x[:, hs, 0:SEQ], l) for x in (q_all, k_all, f_all))
                x, a, b = halves(lev[:, l], l), halves(pre, l), halves(suf, l)
                size = 1 << l
                shape = [P, 2, SEQ // (2 * size), size]
                if l == 0:
                    if p == 0:
                        dve.wait_ge(acc_free, 4 * TPG)
                    else:
                        wait_job(f"os_{p - 1}")
                        dve.wait_ge(drained["act"], drain_of(f"sf_{p - 1}")[1])
                    tt(x[:, :, :, 1], q[:, :, :, 1], f[:, :, :, 1], ALU.mult).then_inc(lev_ready, 1)
                    nc.vector.tensor_copy(x[:, :, :, 0], k[:, :, :, 0]).then_inc(lev_ready, 1)
                    nc.vector.memset(b[:, :, :, 1], 1.0)
                    nc.vector.tensor_copy(b[:, :, :, 0], f[:, :, :, 1])
                    nc.vector.tensor_copy(a[:, :, :, 0], f[:, :, :, 0])
                    link(tt(a[:, :, :, 1], f[:, :, :, 1], f[:, :, :, 0], ALU.mult))
                    return
                left_all = a[:, :, :, 0, size - 1:size].to_broadcast(shape)
                right_all = a[:, :, :, 1, size - 1:size].to_broadcast(shape)
                tt(x[:, :, :, 1], q[:, :, :, 1], a[:, :, :, 1], ALU.mult).then_inc(lev_ready, 1)
                tt(x[:, :, :, 0], k[:, :, :, 0], b[:, :, :, 0], ALU.mult).then_inc(lev_ready, 1)
                dve.wait_ge(lev_ready, 17 * p + 2 * l + 2)
                link(tt(b[:, :, :, 0], b[:, :, :, 0], right_all, ALU.mult))
                if l < LEVELS - 1:
                    link(tt(a[:, :, :, 1], a[:, :, :, 1], left_all, ALU.mult))
                else:
                    tt(k_end, k_all[:, hs, 0:SEQ], suf, ALU.mult).then_inc(lev_ready, 1)

            def head_states(h):
                dve.wait_ge(state_in[h % 2], 16 * (h // 2 + 1))
                for j in range(2):
                    name = f"ou_{h}_{j}"
                    wait_job(name)
                    for bb in range(4):
                        b = 4 * j + bb
                        s = state[:, h % 2, b, :]
                        last = stt(s, s, f_all[:, h, SEQ + b:SEQ + b + 1], bank(name)[:, bb * P:(bb + 1) * P],
                                   ALU.mult, ALU.add)
                    drain(last, name)

            dve.wait_ge(acc_free, G_MAIN * TPG)
            k_s, v_s = k_all[:, :, SEQ:TOK], v_all[:, :, SEQ:TOK]
            nc.vector.tensor_copy(k4[:, :, 0, :], k_s)
            link(nc.vector.tensor_copy(v4[:, :, 0, :], v_s))
            nc.vector.tensor_copy(k4[:, :, 1, :], k4[:, :, 0, :])
            nc.vector.tensor_copy(v4[:, :, 2, :], v4[:, :, 0, :])
            tt(k4[:, :, 2, :], k_s, k4[:, :, 0, :], ALU.subtract)
            tt(k4[:, :, 3, :], k_s, k4[:, :, 0, :], ALU.subtract)
            tt(v4[:, :, 1, :], v_s, v4[:, :, 0, :], ALU.subtract)
            tt(v4[:, :, 3, :], v_s, v4[:, :, 0, :], ALU.subtract).then_inc(kv4_ready, 1)

            def take_scores(p, l):
                name = f"lv_{p}_{l}"
                wait_job(name)
                if l:
                    dve.wait_ge(drained["dve"], drain_of(f"lv_{p}_{l - 1}")[1])
                else:
                    dve.wait_ge(zero_ready, p + 1)
                at = scores[:, 0:2].rearrange("p a h t -> p (a h) t")
                if l == 0:
                    drain(nc.vector.copy_predicated(at, masks[:, 0:P].unsqueeze(1).to_broadcast([P, 4, P]),
                                                    bank(name).rearrange("p (a t) -> p a t", a=4)), name)
                    return
                if l == LEVELS - 1:
                    drain(nc.vector.tensor_copy(at[0:64, :, 64:P], bank(name)[0:64, 0:256].rearrange("p (a k) -> p a k", a=4)),
                          name)
                    return
                n, k = P >> l, 1 << (l - 1)
                mask = masks[:, P + (l - 1) * 64:P + l * 64].rearrange("p (n k) -> p n k", k=k)
                drain(nc.vector.copy_predicated(
                    at.rearrange("p a (n s k) -> p a n s k", s=2, k=k)[:, :, :, 1],
                    mask.unsqueeze(1).to_broadcast([P, 4, n, k]),
                    bank(name)[:, 0:256].rearrange("p (a n k) -> p a n k", a=4, k=k)), name)

            def pair_step(p, n):
                level(p, n)
                if n == 0:
                    wait_job(f"kv_{p}")
                    drain(nc.vector.tensor_copy(
                        kv_smp[:], bank(f"kv_{p}")[0:4 * NSAMP, 0:256].bitcast(F16).rearrange("p (a d) -> p a d", a=4)),
                        f"kv_{p}")
                if n == 6:
                    head_states(2 * p)
                if n >= 3:
                    take_scores(p, n - 3)

            for p in range(PAIRS):
                i = G_MAIN + p

                def finish():
                    if i == 9:
                        for l in range(AHEAD + 2, LEVELS):
                            pair_step(p, l)
                    take_scores(p, 5)
                    if i >= 8:
                        evac_g(i)
                    else:
                        evac_copy(u_all, i, 6)

                group(S_IN, i, finish, S_POOL if i == 9 else None, lambda n: pair_step(p, n))
                take_scores(p, LEVELS - 2)
                take_scores(p, LEVELS - 1)
                head_states(2 * p + 1)
                if p == PAIRS - 1:
                    dve.wait_ge(pd_hi_ready, 1)
                    stt(pd_lo, pd_all, NSCALE, pd_hi, ALU.mult, ALU.subtract).then_inc(pd_ready, 1)
                wait_job(f"os_{p}")
                drain(nc.vector.tensor_copy(o_smp[:, 2 * p:2 * p + 2, :],
                                            bank(f"os_{p}")[:, 0:16].rearrange("p (h b) -> p h b", h=2)), f"os_{p}")
                if p == 2:
                    wait_job("ut_1")
                    u_s = u_all[:, :, SEQ:TOK]
                    link(tt(sb_sum[:], sb_sum[:], u_s, ALU.add))
                    for g, w in enumerate(WINDOWS):
                        s = slice(2 * g, 2 * g + 2)
                        last = stt(u_all[:, s, SEQ:TOK], sb_sum[:, s, :], 1.0 / w, u_all[:, s, SEQ:TOK],
                                   ALU.mult, ALU.subtract)
                    last.then_inc(pd_ready, 1)

            dve.wait_ge(drained["dve"], drain_of(f"os_{PAIRS - 1}")[1])
            tt(o_sq[:], o_smp[:], o_smp[:], ALU.mult).then_inc(osq_ready, 1)
            dve.wait_ge(drained["act"], drain_of(f"o_{PAIRS - 1}")[1])
            link(ts(ss_o[:], ss_o[:], 1.0 / P, EPS, ALU.mult, ALU.add))
            nc.vector.reciprocal(rs_o[:], ss_o[:]).then_inc(mean_ready, 1)
            for j in range(2):
                for b in (2 * j, 2 * j + 1):
                    split(S_OUT, 0, b)
                for n in range(TPG):
                    k = TPG * j + n
                    dve.wait_ge(mix_hi, k + 1)
                    stt(m_lo[:, 8 + k, :], acc[:, n, 0:TOK], ps8[:, k:k + 1], m_hi[:, 8 + k, :],
                        ALU.mult, ALU.subtract).then_inc(acc_free, 1)
            dve.wait_ge(rstd_ready, 3)
            link(newton(rs_o[:], ss_o[:], rt[:].rearrange("p (h a) -> p h a", a=2)))
            for h in range(HEADS):
                for a in range(2):
                    ts(o_tok[:, h, a, :], o_tok[:, h, a, :], rs_o[:, h, a:a + 1], None, ALU.mult).then_inc(xn_o, 1)
            wait_job("oss")
            link(drain(ts(o_ms[:], bank("oss")[:, 0:64].rearrange("p (h b) -> p h b", b=NSAMP), 1.0 / P, EPS,
                          ALU.mult, ALU.add), "oss"))
            nc.vector.reciprocal(o_sq[:], o_ms[:]).then_inc(mean_ready, 1)
            dve.wait_ge(rstd_ready, 4)
            link(newton(o_sq[:], o_ms[:], sb_sum[:]))
            link(tt(o_smp[:], o_smp[:], o_sq[:], ALU.mult))
            link(stt(o_smp[:], o_smp[:], gh8[:, 0:1], sg_all[:, :, SEQ:TOK], ALU.mult, ALU.mult))
            link(nc.vector.tensor_copy(m_hi[:, 0:HEADS, SEQ:TOK], o_smp[:]))
            tt(m_lo[:, 0:HEADS, SEQ:TOK], o_smp[:], m_hi[:, 0:HEADS, SEQ:TOK], ALU.subtract).then_inc(mix_ready, 1)

            for j in range(PAIRS + 1):
                if j < PAIRS:
                    wait_job(f"ot_{j}")
                    if j >= 2:
                        dve.wait_ge(drained["dve"], drain_of(f"ot_{j - 2}")[1])
                    stt((a32, tg32)[j % 2][:, :, 0:SEQ], bank(f"ot_{j}").rearrange("p (h t) -> p h t", h=2), gh8[:, 0:1],
                        sg_all[:, 2 * j:2 * j + 2, 0:SEQ], ALU.mult, ALU.mult).then_inc(mix_tmp, 1)
                if j:
                    q = j - 1
                    dve.wait_ge(mix_tmp, q + 1)
                    dve.wait_ge(mix_hi, 8 + q + 1)
                    drain(tt(m_lo[:, 2 * q:2 * q + 2, 0:SEQ], (a32, tg32)[q % 2][:, :, 0:SEQ],
                             m_hi[:, 2 * q:2 * q + 2, 0:SEQ], ALU.subtract), f"ot_{q}")
            dve.wait_ge(drained["dve"], drain_of(f"ot_{PAIRS - 1}")[1])
            dve.wait_ge(drained["act"], drain_of(f"xt_{KT - 1}")[1])
            nc.vector.memset(h_ssq, 0.0)

            def evac_out(i):
                for n in range(TPG):
                    wait_tile(dve, S_OUT, i, n)
                    h = tile_of(h_all, i, n)
                    stt(h, acc[:, n, 0:TOK], C_N, h, ALU.mult, ALU.add).then_inc(acc_free, 1)
                    dve.wait_ge(acc_free, S_OUT.tile(i, n) + 1)
                    tt(h_sq, h, h, ALU.mult).then_inc(out_chain, 1)
                    dve.wait_ge(out_chain, (i * TPG + n) * 2 + 1)
                    tt(h_ssq, h_ssq, h_sq, ALU.add).then_inc(out_chain, 1)

            with dve.Fori(0, S_OUT.groups - 1) as i:
                group(S_OUT, i, lambda: evac_out(i))
            last_out = S_OUT.groups - 1
            group(S_OUT, last_out, lambda: evac_out(last_out), S_PLE)
            wait_job("hs")
            rstd_row("hs", 5).then_inc(xn_bc, 1)
            for k in range(KT):
                if k % 4 == 0:
                    split(S_FFN, 0, k // 4)
                dve.wait_ge(n_hi_ready, KT + k + 1)
                stt(n_lo[:, k, :], ntmp(k), gf8[:, k:k + 1], n_hi[:, k, :], ALU.mult, ALU.subtract).then_inc(n_ready, 1)

            def evac_ffn(i):
                for n in range(2):
                    dve.wait_ge(gate_ready, i * 2 + (SIG_FFN + n + 1))
                    stt(tg32[:, n, :], acc[:, n, 0:TOK], C_FFN, gate_t[:, n, :], ALU.mult, ALU.mult).then_inc(acc_free, 1)
                dve.wait_ge(acc_free, S_FFN.tile(i, 2))
                for n in range(2):
                    wait_tile(dve, S_FFN, i, 2 + n)
                    stt(a32[:, n, :], acc[:, 2 + n, 0:TOK], C_FFN, tg32[:, n, :], ALU.mult, ALU.mult).then_inc(acc_free, 1)
                dve.wait_ge(acc_free, S_FFN.tile(i, 4))
                fh = ff_hi[:, bass.ds(i * 2, 2), :]
                ts(fh, a32[:], 1.0, None, ALU.mult).then_inc(ffn_chain, 1)
                dve.wait_ge(ffn_chain, i + 1)
                tt(ff_lo[:, bass.ds(i * 2, 2), :], a32[:], fh, ALU.subtract).then_inc(ff_ready, 1)

            dve.wait_ge(buf_stored, 16 * 3)
            with dve.Fori(0, S_FFN.groups - 1) as i:
                group(S_FFN, i, lambda: evac_ffn(i))
            group(S_FFN, S_FFN.groups - 1, lambda: evac_ffn(S_FFN.groups - 1), S_DOWN)
            dve.wait_ge(ff_ready, S_FFN.groups)
            wait_job("es")
            rstd_row("es", 6).then_inc(e_rstd, 1)
            dve.wait_ge(e_rstd, 1)
            nc.vector.memset(h_ssq, 0.0)

            def evac_down(i):
                for n in range(TPG):
                    wait_tile(dve, S_DOWN, i, n)
                    h, nh = tile_of(h_all, i, n), tile_of(n_hi, i, n)
                    stt(h, acc[:, n, 0:TOK], C_FF, h, ALU.mult, ALU.add).then_inc(acc_free, 1)
                    dve.wait_ge(acc_free, S_DOWN.tile(i, n) + 1)
                    ts(nh, h, HSCALE, None, ALU.mult).then_inc(down_chain, 1)
                    dve.wait_ge(down_chain, i * TPG + (n + 1))
                    stt(tile_of(n_lo, i, n), h, HSCALE, nh, ALU.mult, ALU.subtract).then_inc(n_ready, 1)

            with dve.Fori(0, S_DOWN.groups - 1) as i:
                group(S_DOWN, i, lambda: evac_down(i))
            last_down = S_DOWN.groups - 1
            group(S_DOWN, last_down, lambda: evac_down(last_down), S_GATE)

            def evac_gate(i):
                for n in range(TPG):
                    dve.wait_ge(gate_ready, i * TPG + (SIG_GATE + n + 1))
                    h = tile_of(h_all, i, n)
                    stt(tg32[:, 0, :], gate_t[:, n, :], one(g_ple, i, n), tile_of(e_all, i, n),
                        ALU.mult, ALU.mult).then_inc(acc_free, 1)
                    dve.wait_ge(acc_free, S_GATE.tile(i, n) + 1)
                    tt(h, h, tg32[:, 0, :], ALU.add).then_inc(gate_chain, 1)
                    dve.wait_ge(gate_chain, (i * TPG + n) * 3 + 1)
                    tt(h_sq, h, h, ALU.mult).then_inc(gate_chain, 1)
                    dve.wait_ge(gate_chain, (i * TPG + n) * 3 + 2)
                    tt(h_ssq, h_ssq, h_sq, ALU.add).then_inc(gate_chain, 1)

            at, n = VEC_AT["g_ple"]
            g_ple = vec[:, at:at + n]
            group(S_GATE, 0, lambda: (dve.wait_ge(e_ready, 1), evac_gate(0)))
            with dve.Fori(1, S_GATE.groups - 1) as i:
                group(S_GATE, i, lambda: evac_gate(i))
            last_gate = S_GATE.groups - 1
            gf = VEC_AT["g_final"][0]

            def gained(ks):
                for k in ks:
                    ts(h_all[:, k, :], h_all[:, k, :], vec[:, gf + k:gf + k + 1], None, ALU.mult).then_inc(hg_ready, 1)

            def y_part(ks):
                for k in ks:
                    y_out(dve, k, lambda out, src, scale: ts(out, src, scale, None, ALU.mult))

            dve.wait_ge(gate_chain, Y_EARLY * 3)
            for j in range(AHEAD, 8):
                gained(range(3 * (j - AHEAD), 3 * (j - AHEAD) + 3))
                split(S_GATE, last_gate, j)
            y_part(range(0, Y_EARLY, 2))
            evac_gate(last_gate)
            dve.wait_ge(gate_chain, KT * 3)
            gained(range(Y_EARLY, KT))
            wait_job("ys")
            ts(ss[:, 0:2], bank("ys")[:, 0:2], 1.0 / D, EPS, ALU.mult, ALU.add)
            link(drain(ts(ss[0:NSAMP, 2:3], bank("ys")[0:NSAMP, 2:3], 1.0 / D, EPS, ALU.mult, ALU.add), "ys"))
            nc.vector.reciprocal(rs[:], ss[:]).then_inc(mean_ready, 1)
            dve.wait_ge(rstd_ready, 7)
            newton(rs[:], ss[:], rt[:, 0:3]).then_inc(rs_final, 1)
            dve.wait_ge(rs_final, 1)
            dve.wait_ge(drained["act"], drain_of(f"yt_{Y_EARLY - 1}")[1])
            dve.wait_ge(drained["dve"], drain_of(f"yt_{Y_EARLY - 2}")[1])
            ts(y_smp[:, 0:Y_EARLY * P], y_smp[:, 0:Y_EARLY * P], rs[0:NSAMP, 2:3], None, ALU.mult).then_inc(y_scaled, 1)
            ts(y_tok[:, 0, 0:Y_EARLY * P], y_tok[:, 0, 0:Y_EARLY * P], rs[:, 0:1], None, ALU.mult).then_inc(y_scaled, 1)
            y_part(range(Y_EARLY, KT, 2))

        @block.tensor
        def _(pe):
            mm = nc.tensor.matmul

            def stream(st, i, x_hi, x_lo, ready=None, layout=None, sigmoid_frees=False):
                for j in range(st.bpg):
                    pe.wait_ge(lo_done, st.block(i, j) + 1)
                    if ready:
                        ready(j)
                    for n in range(TPG):
                        if j == 0 or st.closed:
                            t = st.tile(i, n, j)
                            if sigmoid_frees:
                                pe.wait_ge(gate_ready, t - (S_GATE.t0 - SIG_GATE) - (TPG - 1))
                            elif not (isinstance(t, int) and t < TPG):
                                pe.wait_ge(acc_free, t - (TPG - 1))
                        out = acc[:, n, 0:TOK]
                        for kk in range(BLOCK_KT):
                            at, kt = layout(j, n, kk) if layout else (kk * COLS + n * P, BLOCK_KT * j + kk)
                            wh = hi[:, st.hl_slot(j), at:at + P]
                            wl = lo[:, st.hl_slot(j), at:at + P]
                            first = kk == 0 and (j == 0 or st.closed)
                            final = kk == BLOCK_KT - 1 and (j == st.bpg - 1 or st.closed)
                            mm(out, wh, x_hi[:, kt, :], start=first, stop=False)
                            mm(out, wh, x_lo[:, kt, :], start=False, stop=False)
                            last = mm(out, wl, x_hi[:, kt, :], start=False, stop=final)
                        if n == TPG - 1:
                            last.then_inc(used, 1)
                        elif final:
                            last.then_inc(acc_done, 1)

            def job(name):
                n = JOB[name]
                if n >= JOB_BANKS:
                    pe.wait_ge(drained[JOBS[n - JOB_BANKS][1]], drained_value(n - JOB_BANKS))
                return wrk[:, n % JOB_BANKS, :]

            def tokens_to_features(out, src, smp, k):
                for a in range(2):
                    nc.tensor.transpose(out[:, a * P:(a + 1) * P], src[:, a, k * P:(k + 1) * P], ident[:])
                return nc.tensor.transpose(out[:, SEQ:TOK], smp[:, k * P:(k + 1) * P], ident[0:NSAMP, 0:NSAMP])

            pe.wait_ge(id_in, 16)
            pe.wait_ge(v_in, 16 * len(VEC_ROWS))
            nc.tensor.transpose(job("vec")[:, 0:NVEC], vec_rows, ident[0:NVEC, 0:NVEC]).then_inc(job_done, 1)
            pe.wait_ge(xn_ready, 2)
            pe.wait_ge(xn_act, 1)

            def n_transposes(c):
                for k in range(4 * c, 4 * c + 4):
                    tokens_to_features(job(f"n1_{k}"), xn_tok, xn_smp, k).then_inc(job_done, 1)

            n_transposes(0)

            def first_jobs(j):
                if j < 3:
                    n_transposes(j + 1)
                if j == 3:
                    pe.wait_ge(p_in, 32)
                    for k in range(2):
                        tokens_to_features(job(f"pt_{k}"), ple_tok, ple_smp, k).then_inc(job_done, 1)
                pe.wait_ge(drained["dve"], drain_of(f"n1_{2 * j + 1}")[1])

            stream(S_IN, 0, n_hi, n_lo, ready=first_jobs)
            with pe.Fori(1, G_MAIN) as i:
                stream(S_IN, i, n_hi, n_lo)
            pe.wait_ge(buf_in, 16)
            out = job("sb")
            for k in range(8):
                last = mm(out[:, k * NSAMP:(k + 1) * NSAMP], buf_tok[:, k * P:(k + 1) * P], win_sel[:, k // 2, :],
                          start=True, stop=True)
            last.then_inc(job_done, 1)
            def sample_kv(p):
                pe.wait_ge(kv4_ready, 1)
                out = job(f"kv_{p}")[0:4 * NSAMP, 0:256].bitcast(F16)
                for n, src in enumerate((k4, k4, v4, v4)):
                    last = nc.tensor.transpose(out[:, n * P:(n + 1) * P],
                                               src[:, 2 * p + n % 2].rearrange("p a b -> p (a b)"), ident16[:])
                last.then_inc(job_done, 1)

            def prompt_v(p):
                out = job(f"vt_{p}")
                for n in range(4):
                    last = nc.tensor.transpose(out[:, n * P:(n + 1) * P],
                                               v_all[:, 2 * p + n // 2, (n % 2) * P:(n % 2 + 1) * P], ident[:])
                last.then_inc(job_done, 1)

            def outer(h):
                pe.wait_ge(kmask_ready, h + 1)
                for j in range(2):
                    out = job(f"ou_{h}_{j}")
                    for bb in range(4):
                        last = mm(out[:, bb * P:(bb + 1) * P], k_mask[:, 4 * j + bb, :], kv_smp[:, 2 + h % 2, :],
                                  start=True, stop=True)
                    last.then_inc(job_done, 1)

            def level_scores(p, l):
                out = job(f"lv_{p}_{l}")
                if l:
                    pe.wait_ge(lev_ready, 17 * p + 2 * l)
                for a in range(2):
                    for h in range(2):
                        s, n = slice(a * P, (a + 1) * P), 2 * a + h
                        if l == 0:
                            last = mm(out[:, n * P:(n + 1) * P], k_all[:, 2 * p + h, s], q_all[:, 2 * p + h, s],
                                      start=True, stop=True)
                            continue
                        x = lev[:, l - 1, h, s]
                        if l == LEVELS - 1:
                            last = mm(out[0:64, n * 64:(n + 1) * 64], x[:, 0:64], x[:, 64:P], start=True, stop=True)
                            continue
                        right = x.rearrange("p (n s k) -> p n s k", s=2, k=1 << (l - 1))[:, :, 1]
                        last = mm(out[:, n * 64:(n + 1) * 64].rearrange("p (n k) -> p n k", k=1 << (l - 1)), x, right,
                                  start=True, stop=True)
                last.then_inc(job_done, 1)

            def pair_jobs(p, j):
                if j == 1:
                    sample_kv(p)
                    prompt_v(p)
                elif j >= 2:
                    level_scores(p, j - 2)
                    if j == 4:
                        outer(2 * p)

            for p in range(PAIRS):
                stream(S_IN, G_MAIN + p, n_hi, n_lo, ready=lambda j: pair_jobs(p, j))
                pair = (2 * p, 2 * p + 1)
                level_scores(p, LEVELS - 2)
                level_scores(p, LEVELS - 1)
                pe.wait_ge(lev_ready, 17 * p + 16)
                out = job(f"cr_{p}")
                for h in range(2):
                    last = mm(out[:, h * P:(h + 1) * P], lev[:, LEVELS - 1, h, 0:P], lev[:, LEVELS - 1, h, P:SEQ],
                              start=True, stop=True)
                last.then_inc(job_done, 1)
                pe.wait_ge(lev_ready, 17 * p + 17)
                out = job(f"ks_{p}")
                for n in range(4):
                    last = nc.tensor.transpose(out[:, n * P:(n + 1) * P], k_end[:, n // 2, (n % 2) * P:(n % 2 + 1) * P],
                                               ident[:])
                last.then_inc(job_done, 1)
                outer(2 * p + 1)
                out = job(f"o_{p}")
                pe.wait_ge(drained["dve"], drain_of(f"lv_{p}_{LEVELS - 1}")[1])
                pe.wait_ge(drained["act"], drain_of(f"ks_{p}")[1])
                for h in range(2):
                    mm(out[:, 2 * h * P:(2 * h + 1) * P], scores[:, 0, h, :], v_tok[:, h, 0, :], start=True, stop=True)
                    o1 = out[:, (2 * h + 1) * P:(2 * h + 2) * P]
                    mm(o1, scores[:, 2, h, :], v_tok[:, h, 0, :], start=True, stop=False)
                    last = mm(o1, scores[:, 1, h, :], v_tok[:, h, 1, :], start=False, stop=True)
                last.then_inc(job_done, 1)
                out = job(f"sf_{p}")
                for h in range(2):
                    mm(out[:, h * P:(h + 1) * P], k_end_tok[:, h, 0, :], v_tok[:, h, 0, :], start=True, stop=False)
                    last = mm(out[:, h * P:(h + 1) * P], k_end_tok[:, h, 1, :], v_tok[:, h, 1, :], start=False, stop=True)
                last.then_inc(job_done, 1)
                out = job(f"os_{p}")
                pe.wait_ge(drained["dve"], drain_of(f"ou_{2 * p + 1}_1")[1])
                for h in range(2):
                    for b in range(NSAMP):
                        n = h * NSAMP + b
                        last = mm(out[:, n:n + 1], state[:, h, b, :], q_all[:, pair[h], SEQ + b:SEQ + b + 1],
                                  start=True, stop=True)
                last.then_inc(job_done, 1)
                if p == 1:
                    pe.wait_ge(acc_free, 8 * TPG)
                    for n in range(2):
                        out = job(f"ut_{n}")
                        for k in range(4):
                            last = nc.tensor.transpose(out[0:POOL_BUF + NSAMP, k * P:(k + 1) * P],
                                                       u_all[:, 4 * n + k, SEQ - POOL_BUF:TOK], ident[:])
                        last.then_inc(job_done, 1)
            pe.wait_ge(pd_ready, 2)
            stream(S_POOL, 0, pd_hi, pd_lo,
                   layout=lambda j, n, kk: ((n // 2 * 2 + kk) * 256 + n % 2 * P, 2 * (2 * j + n // 2) + kk))
            for k in range(KT // 2):
                tokens_to_features(job(f"xt_{k}"), x_tok, x_smp, k).then_inc(job_done, 1)
            out = job("oss")
            pe.wait_ge(osq_ready, 1)
            mm(out[:, 0:64], ones[:], o_sq[:].rearrange("p h b -> p (h b)"), start=True, stop=True).then_inc(job_done, 1)

            def out_jobs(j):
                if j == 0:
                    pe.wait_ge(acc_free, S_POOL.t_end)
                if j in (1, 2):
                    for q in (2 * j - 2, 2 * j - 1):
                        out = job(f"ot_{q}")
                        pe.wait_ge(xn_o, 4 * (q + 1))
                        for n in range(4):
                            last = nc.tensor.transpose(out[:, n * P:(n + 1) * P], o_tok[:, 2 * q + n // 2, n % 2, :], ident[:])
                        last.then_inc(job_done, 1)
                if j == 3:
                    for k in range(KT // 2, KT):
                        tokens_to_features(job(f"xt_{k}"), x_tok, x_smp, k).then_inc(job_done, 1)
                if j == 4:
                    pe.wait_ge(drained["dve"], drain_of(f"ot_{PAIRS - 1}")[1])
                    pe.wait_ge(mix_ready, 1)

            def out_layout(j, n, kk):
                return kk * COLS + n * P, BLOCK_KT * ((j + 4) % 8) + kk

            stream(S_OUT, 0, m_hi, m_lo, ready=out_jobs, layout=out_layout)
            with pe.Fori(1, S_OUT.groups) as i:
                stream(S_OUT, i, m_hi, m_lo, layout=out_layout)

            def sum_h(j):
                if j == 1:
                    out = job("hs")
                    pe.wait_ge(out_chain, 2 * KT)
                    mm(out[:, 0:TOK], ones[:], h_ssq, start=True, stop=True).then_inc(job_done, 1)

            stream(S_PLE, 0, pt_hi, pt_lo, ready=sum_h, layout=lambda j, n, kk: (kk * COLS + n * P, kk))
            with pe.Fori(0, S_FFN.groups) as i:
                stream(S_FFN, i, n_hi, n_lo, ready=lambda j: pe.wait_ge(n_ready, 2 * j + 2))
            out = job("es")
            pe.wait_ge(esum_ready, 1)
            mm(out[:, 0:TOK], ones[:], e_sq[:, 0:TOK], start=True, stop=True).then_inc(job_done, 1)
            with pe.Fori(0, S_DOWN.groups) as i:
                stream(S_DOWN, i, ff_hi, ff_lo, ready=lambda j: pe.wait_ge(ff_ready, j + 1))
            def y_transposes(ks):
                for k in ks:
                    out = job(f"yt_{k}")
                    pe.wait_ge(hg_ready, k + 1)
                    for a in range(2):
                        nc.tensor.transpose(out[:, a * P:(a + 1) * P], h_all[:, k, a * P:(a + 1) * P], ident[:])
                    nc.tensor.transpose(out[0:NSAMP, SEQ:SEQ + P], h_all[:, k, SEQ:TOK], ident[:]).then_inc(job_done, 1)

            stream(S_GATE, 0, n_hi, n_lo, ready=lambda j: pe.wait_ge(n_ready, KT + 2 * j + 2))
            with pe.Fori(1, S_GATE.groups - 1) as i:
                stream(S_GATE, i, n_hi, n_lo, sigmoid_frees=True)
            stream(S_GATE, S_GATE.groups - 1, n_hi, n_lo, sigmoid_frees=True,
                   ready=lambda j: y_transposes(range(3 * j - 12, 3 * j - 9)) if j >= 4 else None)
            out = job("ys")
            pe.wait_ge(gate_chain, KT * 3)
            for n in range(3):
                m = P if n < 2 else NSAMP
                last = mm(out[0:m, n:n + 1], h_ssq[:, n * P:n * P + m], ones[:, 0:1], start=True, stop=True)
            last.then_inc(job_done, 1)
            y_transposes(range(Y_EARLY, KT))


_INS = ["x_prompt", "x_sample", "state_hgrn", "state_pool", "p_prompt", "p_sample", "g_mix", "w_in", "lb_logits",
        "g_head", "w_pool", "pool_scale", "w_out", "g_ffn", "w_gate_up", "w_down", "w_ple", "g_ple", "w_ple_gate",
        "g_final"]
_OUTS = [("y_prompt", (1, SEQ, D)), ("y_sample", (NSAMP, 1, D)), ("new_hgrn_prompt", (1, 1, HEADS, DK, P)),
         ("new_pool_prompt", (1, 1, POOL_BUF, 1024)), ("new_hgrn_sample", (1, NSAMP, HEADS, DK, P)),
         ("new_pool_sample", (1, NSAMP, POOL_BUF, 1024))]


def _constants():
    s, t = np.arange(P)[:, None], np.arange(P)[None, :]
    masks = [s == t]
    for l in range(LEVELS - 1):
        right = t[:, (t[0] >> l) % 2 == 1]
        masks.append((s >> (l + 1) == right >> (l + 1)) & ((s >> l) % 2 == 0))
    masks = np.concatenate(masks, 1).astype(np.float32)
    delta = np.tile(np.eye(NSAMP, dtype=np.float32), (4, 1))
    rcnt = np.zeros((P, 4, 16), np.float32)
    win = np.zeros((NSAMP, POOL_BUF, 4, NSAMP), np.float32)
    for g, w in enumerate(WINDOWS):
        rcnt[:, g] = 1.0 / np.minimum(np.arange(16) + 1, w)
        for b in range(NSAMP):
            win[b, POOL_BUF - (w - 1):, g, b] = 1.0
    return {"c_ident": np.eye(P, dtype=np.float32), "c_masks": masks, "c_rcnt": rcnt, "c_delta": delta,
            "c_win": win.reshape(NSAMP * POOL_BUF, 4, NSAMP)}


def kernel(**inputs):
    import concourse.bacc as _bacc
    from concourse.bass_utils import run_bass_kernel_spmd as _run

    nc = _bacc.Bacc("TRN2", target_bir_lowering=False, num_devices=1)
    arrays, io = {}, {}
    given = {n: np.ascontiguousarray(inputs[n]) for n in _INS} | _constants()
    for name, a in given.items():
        arrays[f"in_{name}_dram"] = a
        io[name] = nc.dram_tensor(f"in_{name}_dram", a.shape, mybir.dt.from_np(a.dtype), kind="ExternalInput").ap()
    for name, shape in _OUTS:
        io[name] = nc.dram_tensor(f"out_{name}_dram", shape, F32, kind="ExternalOutput").ap()
    build(nc, io)
    r = _run(nc, [arrays], core_ids=[0])
    return tuple(r.results[0][f"out_{name}_dram"] for name, _ in _OUTS)
```
